# Optimizing a Trainium2 kernel written in Bass

```python
import jax, jax.numpy as jnp
from jax import lax
import numpy as np

D_MODEL = 1024
BATCH = 1
SEQ = 512
DEPTH = 1

CHUNK = 128
A_HEADS = 4
A_HEAD_DIM = 128
A_WIDTH = A_HEADS * A_HEAD_DIM
POOL_WINDOWS = (2, 4, 8, 16)
B_GROUP_DIM = 128
B_WIDTH = len(POOL_WINDOWS) * B_GROUP_DIM
C_WIDTH = 512
CONV_WIDTH = 3
N_BRANCH = 3
IN_SPLIT_SIZES = (A_WIDTH, A_WIDTH, B_WIDTH, C_WIDTH, C_WIDTH, C_WIDTH, N_BRANCH * D_MODEL)
IN_COLS = sum(IN_SPLIT_SIZES)
_FF_RAW = -(-8 * D_MODEL // 3)
D_FF = -(-_FF_RAW // 256) * 256
N_MOD = 6
EPS = 1e-6

kernel_name = "hybrid_gmlp_pool_conv_gated_trunk"

def rmsnorm(x, g):
    xf = x.astype(jnp.float32)
    xf = xf * lax.rsqrt(jnp.mean(xf * xf, axis=-1, keepdims=True) + EPS)
    return xf.astype(x.dtype) * g

def layernorm(x, g, b):
    xf = x.astype(jnp.float32)
    mu = jnp.mean(xf, axis=-1, keepdims=True)
    var = jnp.mean(jnp.square(xf - mu), axis=-1, keepdims=True)
    return ((xf - mu) * lax.rsqrt(var + EPS)).astype(x.dtype) * g + b

def modulate(h, shift, scale):
    return h * (1.0 + scale[:, None, :]) + shift[:, None, :]

def split_cols(z):
    parts, off = [], 0
    for n in IN_SPLIT_SIZES:
        parts.append(z[..., off:off + n])
        off += n
    return parts

def gmlp_branch(u, v, ln_g, ln_b, w_s, b_s):
    bsz, seq, _ = v.shape
    v = layernorm(v, ln_g, ln_b)
    vc = v.reshape(bsz, seq // CHUNK, CHUNK, A_HEADS, A_HEAD_DIM)
    mask = jnp.tril(jnp.ones((CHUNK, CHUNK), dtype=w_s.dtype))
    w = w_s * mask[None]
    s = jnp.einsum('hts,bnshd->bnthd', w, vc) + jnp.transpose(b_s)[None, None, :, :, None]
    return u * s.reshape(bsz, seq, A_WIDTH)

def pool_branch(xb, pool_w, pool_scale):
    bsz, seq, _ = xb.shape
    xf = xb.astype(jnp.float32)
    cs = jnp.pad(jnp.cumsum(xf, axis=1), ((0, 0), (1, 0), (0, 0)))
    pos = jnp.arange(seq)
    outs = []
    for g, win in enumerate(POOL_WINDOWS):
        sl = slice(g * B_GROUP_DIM, (g + 1) * B_GROUP_DIM)
        csg = cs[..., sl]
        lag = jnp.pad(csg, ((0, 0), (win - 1, 0), (0, 0)))[:, :seq]
        cnt = jnp.minimum(pos + 1, win).astype(jnp.float32)[None, :, None]
        outs.append((csg[:, 1:] - lag) / cnt - xf[..., sl])
    p = jnp.stack(outs, axis=2).astype(xb.dtype)
    y = jnp.einsum('bsgc,gcd->bsgd', p, pool_w).reshape(bsz, seq, B_WIDTH)
    return y * pool_scale

def conv_branch(bg, cg, h, conv_w):
    seq = h.shape[1]
    z = cg * h
    zp = jnp.pad(z, ((0, 0), (CONV_WIDTH - 1, 0), (0, 0)))
    y = conv_w[0] * zp[:, 0:seq]
    for k in range(1, CONV_WIDTH):
        y = y + conv_w[k] * zp[:, k:k + seq]
    return bg * y

def setup_inputs(seed: int = 0) -> dict:
    key = jax.random.key(seed)
    ks = jax.random.split(key, 24)
    f32 = jnp.float32
    nrm = lambda k, shape, scale: (jax.random.normal(k, shape, f32) * scale).astype(f32)
    L, D = DEPTH, D_MODEL
    return {
        "x": nrm(ks[0], (BATCH, SEQ, D), 1.0),
        "c": nrm(ks[1], (BATCH, D), 1.0),
        "w_mod": nrm(ks[2], (L, D, N_MOD * D), 0.5 * D ** -0.5),
        "b_mod": nrm(ks[3], (L, N_MOD * D), 0.02),
        "g_mix": 1.0 + nrm(ks[4], (L, D), 0.05),
        "w_in": nrm(ks[5], (L, D, IN_COLS), D ** -0.5),
        "gm_ln_g": 1.0 + nrm(ks[6], (L, A_WIDTH), 0.05),
        "gm_ln_b": nrm(ks[7], (L, A_WIDTH), 0.02),
        "gm_w_s": nrm(ks[8], (L, A_HEADS, CHUNK, CHUNK), CHUNK ** -0.5),
        "gm_b_s": 1.0 + nrm(ks[9], (L, A_HEADS, CHUNK), 0.05),
        "w_pa": nrm(ks[10], (L, A_WIDTH, D), A_WIDTH ** -0.5),
        "pool_w": nrm(ks[11], (L, len(POOL_WINDOWS), B_GROUP_DIM, B_GROUP_DIM), B_GROUP_DIM ** -0.5),
        "pool_scale": 1.0 + nrm(ks[12], (L, B_WIDTH), 0.1),
        "w_pb": nrm(ks[13], (L, B_WIDTH, D), B_WIDTH ** -0.5),
        "conv_w": nrm(ks[14], (L, CONV_WIDTH, C_WIDTH), CONV_WIDTH ** -0.5),
        "w_pc": nrm(ks[15], (L, C_WIDTH, D), C_WIDTH ** -0.5),
        "w_o": nrm(ks[16], (L, D, D), D ** -0.5),
        "g_ffn": 1.0 + nrm(ks[17], (L, D), 0.05),
        "w_13": nrm(ks[18], (L, D, 2 * D_FF), D ** -0.5),
        "w_2": nrm(ks[19], (L, D_FF, D), D_FF ** -0.5),
        "g_final": 1.0 + nrm(ks[20], (D,), 0.05),
    }

def reference(x, c, w_mod, b_mod, g_mix, w_in, gm_ln_g, gm_ln_b, gm_w_s, gm_b_s, w_pa,
              pool_w, pool_scale, w_pb, conv_w, w_pc, w_o, g_ffn, w_13, w_2, g_final):
    bsz, seq, d = x.shape
    c_act = jax.nn.silu(c)
    for l in range(DEPTH):
        mod = (c_act @ w_mod[l] + b_mod[l]).reshape(bsz, N_MOD, d)
        shift1, scale1, gate1 = mod[:, 0], mod[:, 1], mod[:, 2]
        shift2, scale2, gate2 = mod[:, 3], mod[:, 4], mod[:, 5]

        h = modulate(rmsnorm(x, g_mix[l]), shift1, scale1)
        z = h @ w_in[l]
        u_a, v_a, x_b, bg_c, cg_c, h_c, gate_logits = split_cols(z)
        y_a = gmlp_branch(jax.nn.gelu(u_a), jax.nn.gelu(v_a), gm_ln_g[l], gm_ln_b[l],
                          gm_w_s[l], gm_b_s[l]) @ w_pa[l]
        y_b = pool_branch(x_b, pool_w[l], pool_scale[l]) @ w_pb[l]
        y_c = conv_branch(bg_c, cg_c, h_c, conv_w[l]) @ w_pc[l]
        g = jax.nn.sigmoid(gate_logits).reshape(bsz, seq, N_BRANCH, d)
        merged = g[:, :, 0] * y_a + g[:, :, 1] * y_b + g[:, :, 2] * y_c
        x = x + gate1[:, None, :] * (merged @ w_o[l])

        h = modulate(rmsnorm(x, g_ffn[l]), shift2, scale2)
        ab = h @ w_13[l]
        a, b = ab[..., :D_FF], ab[..., D_FF:]
        x = x + gate2[:, None, :] * ((jax.nn.silu(a) * b) @ w_2[l])
    return rmsnorm(x, g_final)


_drawn_inputs = setup_inputs


def setup_inputs(seed=0):
    import zlib

    import numpy as np

    out = dict(_drawn_inputs(seed))
    spreads = {}
    factors = {'gm_ln_g': 8.0, 'gm_ln_b': 42.775, 'gm_b_s': 8.0, 'pool_scale': 3.924, 'g_ffn': 4.259}
    for name, (base, spread) in spreads.items():
        noise = np.random.default_rng([zlib.crc32(name.encode()), seed]).standard_normal(out[name].shape)
        drawn = base * np.exp(spread * noise) if base else spread * noise
        out[name] = __import__('jax').numpy.asarray(drawn.astype(out[name].dtype))
    for name, factor in factors.items():
        out[name] = (out[name] * factor).astype(out[name].dtype)
    return out
```

```python
import concourse.bass as bass
from concourse import mybir
from contextlib import ExitStack

fp32 = mybir.dt.float32
fp32r = mybir.dt.float32r
ALU = mybir.AluOpType
ACT = mybir.ActivationFunctionType

P = 128
D = 1024
SEQ = 512
TT = SEQ // P
KD = D // P
HEADS = 4
WIDTH = 512
KW = WIDTH // P
WINDOWS = (2, 4, 8, 16)
DFF = 2816
KF = DFF // P
EPS = 1e-6
RING = 4
SLOT = 1024
BIG = 3 * KW * P
PAD = 16

COL_U, COL_V, COL_XB, COL_BG, COL_CG, COL_HC, COL_GATE = 0, 512, 1024, 1536, 2048, 2560, 3072

N_A = 0
N_U0 = N_A + KD
N_XB = N_U0 + 1
N_CONV = N_XB + 4
N_C = N_CONV + 12
N_WO = N_C + 4 * KD
N_UP = N_WO + KD
N_DOWN = N_UP + 2 * KF
N_END = N_DOWN + KF
AHEAD = 2

V_C, V_GMIX, V_GFFN, V_PSC, V_CONV, V_LNG, V_LNB, V_END = 0, 8, 16, 24, 28, 40, 44, 48

YA, YB, YC, MERGED = 0, 4, 8, 12


def slot_at(n):
    s = n % RING
    return 0 if s == 0 else BIG + SLOT * (s - 1)


def build(nc, x, c, w_mod, b_mod, g_mix, w_in, gm_ln_g, gm_ln_b, gm_w_s, gm_b_s, w_pa, pool_w,
          pool_scale, w_pb, conv_w, w_pc, w_o, g_ffn, w_13, w_2, g_final, out):
    ctx = ExitStack()
    with ctx:
        def sb(name, shape, dt=fp32):
            return ctx.enter_context(nc.sbuf_tensor(name, shape, dt))

        def sem(name):
            return ctx.enter_context(nc.semaphore(name))

        x_tok = sb("x_tok", [P, TT, D])
        raw_w = sb("raw_w", [P, BIG + 3 * SLOT])
        w_hi = sb("w_hi", [P, BIG + 3 * SLOT], fp32r)
        w_lo = sb("w_lo", [P, BIG + 3 * SLOT], fp32r)
        h_hi = sb("h_hi", [P, KD, SEQ], fp32r)
        h_lo = sb("h_lo", [P, KD, SEQ], fp32r)
        act_hi = sb("act_hi", [P, KF, SEQ], fp32r)
        act_lo = sb("act_lo", [P, KF, SEQ], fp32r)
        mod_w = sb("mod_w", [P, 4 * 1024])
        mod_b = sb("mod_b", [P, 2, 256])
        mod_acc = sb("mod_acc", [P, 2, 256])
        pads = sb("pads", [P, 3, PAD + SEQ])
        tmp = sb("tmp", [P, D])
        ident = sb("ident", [P, P])
        ones = sb("ones", [P, P])
        rows = sb("rows", [P, P])
        vec = sb("vec", [P, V_END])
        c_act = sb("c_act", [P, KD])
        a1 = sb("a1", [P, KD])
        b1 = sb("b1", [P, KD])
        cols2 = sb("cols2", [P, 2, KD])
        a2 = sb("a2", [P, KD])
        recip = sb("recip", [P, PAD])
        half = sb("half", [P, TT])
        ssq = sb("ssq", [P, 3, TT])
        ms = sb("ms", [P, 4, TT])
        rstd = sb("rstd", [P, 4, TT])
        stats = sb("stats", [P, TT, 6])
        mv = sb("mv", [P, TT, 2])
        fix = sb("fix", [P, PAD])

        ws_raw = mod_w[:, 0:512]
        ws_t = mod_w[:, 512:1024]
        bs_row = mod_w[:, 1024:1536]
        gate_bias = mod_w[:, 1536:2048]
        pool_sb = mod_w[:, 2048:2560]
        cg_sb = mod_w[:, 2560:3072]
        taps = mod_w[:, 3072:3584]
        yc_sb = mod_w[:, 3584:4096]
        gate_row = [mod_w[:, 2048:3072], mod_w[:, 3072:4096]]
        h2_tmp = mod_w[:, 0:1024]
        gfin_row = mod_w[:, 1024:2048]
        x1n = [mod_w[:, 1024:2048], pads[:, :, :].rearrange("p a b -> p (a b)")[:, 0:D]]
        flat_x = x_tok[:, :, :].rearrange("p t d -> p (t d)")
        v_tok = [flat_x[:, i * 512:(i + 1) * 512] for i in range(4)]
        u_gelu = [flat_x[:, 2048 + i * 512:2048 + (i + 1) * 512] for i in range(4)]
        sig = [flat_x[:, i * 512:(i + 1) * 512] for i in range(3)]
        merge = [flat_x[:, 1536 + i * 512:1536 + (i + 1) * 512] for i in range(2)]

        ps = [ctx.enter_context(nc.psum_tensor(f"bank{i}", [P, 512], fp32)) for i in range(8)]

        s_x = [sem(f"x_landed{t}") for t in range(TT)]
        s_vec = sem("vectors_landed")
        s_small = sem("branch_weights_landed")
        s_gfin = sem("gfinal_landed")
        s_raw = [sem(f"raw_landed{i}") for i in range(RING)]
        s_mod = [sem(f"mod_landed{i}") for i in range(2)]
        s_out = sem("out_stored")
        s_const = sem("constants_ready")
        s_zero = sem("zeros_ready")
        s_whi = sem("slab_hi_ready")
        s_wlo = sem("slab_lo_ready")
        s_used = sem("slab_used")
        s_vect = sem("vectors_transposed")
        s_vecsb = sem("vectors_in_sbuf")
        s_c = sem("c_act_ready")
        s_ssq = sem("squares_summed")
        s_ms = sem("mean_squares_ready")
        s_rstd = sem("rstd_ready")
        s_xn = sem("x_normed")
        s_xt = sem("x_transposed")
        s_xta = sem("x_transposed_copied_act")
        s_xtd = sem("x_transposed_copied_dve")
        s_acc = sem("mod_accumulated")
        s_red = sem("mod_reduced")
        s_ab = sem("mod_columns_read")
        s_row = sem("mod_gate_row_copied")
        s_h = sem("h_fp32_ready")
        s_hhi = sem("h_hi_ready")
        s_hlo = sem("h_lo_ready")
        s_vg = sem("v_gelu_ready")
        s_ug = sem("u_gelu_ready")
        s_mv = sem("ln_stats_ready")
        s_lnr = sem("ln_rstd_ready")
        s_vn = sem("v_normed")
        s_mask = sem("ws_masked")
        s_wst = sem("ws_transposed")
        s_wsc = sem("ws_transposed_copied")
        s_rs = sem("ws_rowsums_ready")
        s_gb = sem("gate_bias_ready")
        s_first = sem("first_stage_tile_ready")
        s_gm = sem("gating_matmuls_done")
        s_gmr = sem("gating_read")
        s_ya = sem("y_a_ready")
        s_yahi = sem("y_a_hi_ready")
        s_xb = sem("xb_copied")
        s_p = sem("pooled_ready")
        s_pm = sem("pool_map_ready")
        s_ybhi = sem("y_b_hi_ready")
        s_yblo = sem("y_b_lo_ready")
        s_cg = sem("cg_copied")
        s_z = sem("hc_read")
        s_yc = sem("y_c_ready")
        s_ychi = sem("y_c_hi_ready")
        s_yclo = sem("y_c_lo_ready")
        s_sig = sem("gate_sigmoid_ready")
        s_y = sem("branch_products_read")
        s_m = sem("merged_ready")
        s_mhi = sem("merged_hi_ready")
        s_mlo = sem("merged_lo_ready")
        s_wo = sem("mixed_ready")
        s_x1 = sem("x1_ready")
        s_x1n = sem("x1_normed")
        s_x1t = sem("x1_transposed")
        s_h2a = sem("h2_read_act")
        s_h2d = sem("h2_read_dve")
        s_h2hi = sem("h2_hi_ready")
        s_h2lo = sem("h2_lo_ready")
        s_a = sem("silu_ready")
        s_g = sem("hidden_ready")
        s_ghi = sem("hidden_hi_ready")
        s_glo = sem("hidden_lo_ready")
        s_yp = sem("branch_projected")
        s_dn = sem("ffn_out_ready")
        s_x2 = sem("x2_ready")
        s_o = sem("out_ready")
        s_dve = sem("vector_step")

        w_in_k = w_in.rearrange("(k p) n -> p k n", p=P)
        w_mod_k = w_mod.rearrange("(k p) n -> p k n", p=P)
        w_13_k = w_13.rearrange("(k p) n -> p k n", p=P)
        w_p_k = [w.rearrange("(k p) n -> p k n", p=P) for w in (w_pa, w_pb, w_pc)]

        def raw(n, width=SLOT):
            return raw_w[:, slot_at(n):slot_at(n) + width]

        def hi(n, width=SLOT):
            return w_hi[:, slot_at(n):slot_at(n) + width]

        def lo(n, width=SLOT):
            return w_lo[:, slot_at(n):slot_at(n) + width]

        def mod_slot(i):
            return mod_w[:, i * 2048:(i + 1) * 2048].rearrange("p (k m n) -> p k m n", k=KD, m=2)

        block = ctx.enter_context(nc.Block())

        @block.sync
        def _(sp):
            def early(*values):
                for v in values:
                    sp.compute_val(v)

            def load(n, dst, src, it=None, step=RING):
                if n >= RING:
                    sp.wait_ge(s_wlo, n - 3 if it is None else it * step + (n - 3))
                return sp.dma_start(dst, src)

            def load_cols(n, w_k, col, it=None, step=RING):
                if it is not None:
                    early(col * 4, it * step + (n - 3))
                load(n, raw(n).rearrange("p (k n) -> p k n", k=KD), w_k[:, :, bass.ds(col, P)],
                     it, step).then_inc(s_raw[n % RING], 16)

            def load_rows(n, w, k):
                load(n, raw(n), w[k * P:(k + 1) * P, :]).then_inc(s_raw[n % RING], 16)

            def load_mod(buf, bias, col0, col1):
                for m, col in enumerate((col0, col1)):
                    sp.dma_start(mod_slot(buf)[:, :, m, :], w_mod_k[:, :, bass.ds(col, P)])\
                        .then_inc(s_mod[bias], 16)
                    sp.dma_start(mod_b[0:1, bias, m * P:(m + 1) * P],
                                 b_mod[:, bass.ds(col, P)]).then_inc(s_mod[bias], 16)

            for t in range(TT):
                sp.dma_start(x_tok[:, t, :], x[t * P:(t + 1) * P, :]).then_inc(s_x[t], 16)
            sp.wait_ge(s_zero, 1)
            for k in range(KD):
                if k >= 2:
                    sp.wait_ge(s_acc, k - 1)
                    sp.wait_ge(s_red, k - 1)
                load_mod(k % 2, k % 2, D + k * P, k * P)
                load(k, raw(k)[:, 0:896], w_in[k * P:(k + 1) * P, 128:1024]).then_inc(s_raw[k % RING], 16)
            load_cols(N_U0, w_in_k, COL_U)
            load_cols(N_XB, w_in_k, COL_XB)
            load_cols(N_XB + 1, w_in_k, COL_XB + P)
            sp.wait_ge(s_acc, KD)
            sp.dma_start(ws_raw.rearrange("p (h s) -> p h s", h=HEADS),
                         gm_w_s.rearrange("h t s -> t h s")).then_inc(s_small, 16)
            sp.dma_start(pool_sb.rearrange("p (g d) -> p g d", g=4),
                         pool_w.rearrange("g c d -> c g d")).then_inc(s_small, 16)
            sp.dma_start(bs_row, gm_b_s.rearrange("(o h) t -> o (h t)", o=1).broadcast_to((P, HEADS * P)))\
                .then_inc(s_small, 16)
            for g in range(2, 4):
                load_cols(N_XB + g, w_in_k, COL_XB + g * P)
            for cc in range(4):
                load_cols(N_CONV + 3 * cc, w_in_k, COL_CG + cc * P)
                load_cols(N_CONV + 3 * cc + 1, w_in_k, COL_HC + cc * P)
                load_cols(N_CONV + 3 * cc + 2, w_in_k, COL_BG + cc * P)

            def load_branch(j, it=None):
                n = N_C + 3
                if it is not None:
                    early(j * 4, it * 4 + (n - 3))
                sp.wait_ge(s_wlo, n - 3 if it is None else it * 4 + (n - 3))
                for b in range(3):
                    sp.dma_start(raw(n, BIG)[:, b * 512:(b + 1) * 512].rearrange("p (k n) -> p k n", k=KW),
                                 w_p_k[b][:, :, bass.ds(j, P)]).then_inc(s_raw[n % RING], 16)

            for b in range(3):
                load_cols(N_C + b, w_in_k, COL_GATE + b * D)
            load_branch(0)
            sp.wait_ge(s_gmr, HEADS)
            with sp.Fori(1, KD) as j:
                load_cols(N_C, w_in_k, j * P + COL_GATE, j)
                cols = [j * P + (i * D - P) for i in (2, 3, 4, 5)]
                need = [2 * j + (KD - i) for i in (3, 2, 1)]
                early(*[4 * v for v in cols], *need)
                sp.wait_ge(s_acc, need[1])
                sp.wait_ge(s_red, need[0])
                load_mod(0, 0, cols[0], cols[1])
                load_cols(N_C + 1, w_in_k, j * P + (COL_GATE + D), j)
                load_cols(N_C + 2, w_in_k, j * P + (COL_GATE + 2 * D), j)
                sp.wait_ge(s_acc, need[2])
                sp.wait_ge(s_red, need[1])
                load_mod(0, 1, cols[2], cols[3])
                load_branch(j * P, j)
            load_rows(N_WO, w_o, 0)
            sp.wait_ge(s_acc, 3 * KD - 2)
            sp.wait_ge(s_red, 3 * KD - 3)
            load_mod(0, 0, 3 * D - P, 4 * D - P)
            load_rows(N_WO + 1, w_o, 1)
            load_rows(N_WO + 2, w_o, 2)
            sp.wait_ge(s_acc, 3 * KD - 1)
            sp.wait_ge(s_red, 3 * KD - 2)
            load_mod(0, 1, 5 * D - P, 6 * D - P)
            for k in range(3, 6):
                load_rows(N_WO + k, w_o, k)
            sp.wait_ge(s_mlo, KD)
            sp.wait_ge(s_mhi, KD)
            for t in range(TT):
                sp.dma_start(x_tok[:, t, :], x[t * P:(t + 1) * P, :]).then_inc(s_x[t], 16)
            for k in range(6, KD):
                load_rows(N_WO + k, w_o, k)
            with sp.Fori(0, KF // 2) as i:
                for f in range(2):
                    for m in range(2):
                        load_cols(N_UP + 2 * f + m, w_13_k, i * (2 * P) + (m * DFF + f * P), i)
            sp.wait_ge(s_x1t, 2 * TT)
            sp.dma_start(gfin_row, g_final.rearrange("(o n) -> o n", o=1).broadcast_to((P, D))).then_inc(s_gfin, 16)
            for k in range(KF):
                load_rows(N_DOWN + k, w_2, k)
            for t in range(TT):
                for q in range(2):
                    sp.wait_ge(s_o, 2 * t + q + 1)
                    sp.dma_start(out[t * P:(t + 1) * P, q * 512:(q + 1) * 512],
                                 x_tok[:, t, q * 512:(q + 1) * 512]).then_inc(s_out, 16)
            sp.wait_ge(s_out, 16 * 2 * TT)

        @block.gpsimd
        def _(pool):
            nc.gpsimd.memset(mod_b[:, :, :], 0.0).then_inc(s_zero, 1)
            nc.gpsimd.memset(ident[:, :], 0.0).then_inc(s_zero, 1)
            pool.wait_ge(s_zero, 2)
            nc.gpsimd.affine_select(out=ident[:, :], in_=ident[:, :], compare_op=ALU.not_equal, fill=1.0,
                                    base=0, pattern=[[-1, P]], channel_multiplier=1).then_inc(s_const, 1)
            nc.gpsimd.memset(half[:, :], -0.5)
            nc.gpsimd.memset(ones[:, :], 1.0)
            nc.gpsimd.memset(pads[:, :, 0:PAD], 0.0)
            for i in range(PAD):
                last = nc.gpsimd.memset(recip[:, i:i + 1], 1.0 / (i + 1))
            last.then_inc(s_const, 1)
            pool.wait_ge(s_const, 2)
            steps = 0

            def inverse_root(i, t, width, source, scale):
                nonlocal steps
                nc.gpsimd.tensor_scalar(ms[:, i, t:t + width], source, scale, EPS, ALU.mult, ALU.add)\
                    .then_inc(s_ms, 1)
                steps += 1
                pool.wait_ge(s_ms, steps)
                return nc.gpsimd.tensor_tensor(rstd[:, i, t:t + width], ms[:, i, t:t + width],
                                               half[:, t:t + width], ALU.pow)

            for t in range(TT):
                pool.wait_ge(s_ssq, t + 1)
                inverse_root(0, t, 1, ssq[:, 0, t:t + 1], 1.0 / D).then_inc(s_rstd, 1)
            pool.wait_ge(s_small, 48)
            nc.gpsimd.affine_select(out=ws_raw.rearrange("p (h s) -> p h s", h=HEADS),
                                    in_=ws_raw.rearrange("p (h s) -> p h s", h=HEADS),
                                    compare_op=ALU.is_ge, fill=0.0, base=0,
                                    pattern=[[0, HEADS], [-1, P]], channel_multiplier=1).then_inc(s_mask, 1)
            pool.wait_ge(s_mv, TT)
            inverse_root(1, 0, TT, mv[:, :, 1], 1.0).then_inc(s_lnr, 1)
            for i, base in ((1, TT), (2, 2 * TT)):
                for t in range(TT):
                    pool.wait_ge(s_ssq, base + t + 1)
                    inverse_root(i + 1, t, 1, ssq[:, i, t:t + 1], 1.0 / D).then_inc(s_rstd, 1)

        @block.scalar
        def _(act):
            def split_hi(n, it=None, step=RING, width=SLOT):
                big = n >= N_C + 3 and n <= N_WO - 1 and (n - N_C) % 4 == 3
                s = n % RING
                before = 16 * (n // RING + 1)
                each = 16
                if s == 0:
                    first = (N_C + 3) // RING
                    extra = min(max(n // RING + 1 - first, 0), KD) * 32
                    before += extra
                    if it is not None and big:
                        each = 48
                act.wait_ge(s_raw[s], before if it is None else it * each + before)
                if n >= RING:
                    act.wait_ge(s_used, n - 3 if it is None else it * step + (n - 3))
                nc.scalar.activation(hi(n, width), raw(n, width), ACT.Copy).then_inc(s_whi, 1)

            for dst, src in ((V_C, c.rearrange("o (k p) -> (o k) p", p=P)),
                             (V_GMIX, g_mix.rearrange("o (k p) -> (o k) p", p=P)),
                             (V_GFFN, g_ffn.rearrange("o (k p) -> (o k) p", p=P)),
                             (V_PSC, pool_scale.rearrange("o (k p) -> (o k) p", p=P)),
                             (V_CONV, conv_w.rearrange("w (k p) -> (w k) p", p=P)),
                             (V_LNG, gm_ln_g.rearrange("o (k p) -> (o k) p", p=P)),
                             (V_LNB, gm_ln_b.rearrange("o (k p) -> (o k) p", p=P))):
                act.dma_start(rows[dst:dst + src.shape[0], :], src).then_inc(s_vec, 16)
            act.wait_ge(s_vecsb, 1)
            nc.scalar.activation(c_act[:, :], vec[:, V_C:V_C + KD], ACT.Silu).then_inc(s_c, 1)

            def square(t, i):
                if t >= 1:
                    act.wait_ge(s_ssq, t)
                nc.scalar.activation(tmp[:, :], x_tok[:, t, :], ACT.Square,
                                     accum_out=ssq[:, i, t:t + 1]).then_inc(s_ssq, 1)

            def x_copy(t):
                act.wait_ge(s_xt, 2 * t + 1)
                nc.scalar.activation(x_tok[:, t, 0:512], ps[2 * (t % 3)][:, :], ACT.Copy).then_inc(s_xta, 1)

            for t in range(TT):
                act.wait_ge(s_x[t], 16)
                square(t, 0)
                if t >= 2:
                    x_copy(t - 2)
            x_copy(2)
            split_hi(0, width=896)
            x_copy(3)

            def h_block(k):
                act.wait_ge(s_ab, k + 1)
                act.wait_ge(s_xtd, TT)
                act.wait_ge(s_xta, TT)
                if k >= 2:
                    act.wait_ge(s_hlo, k - 1)
                buf = tmp[:, (k % 2) * 512:(k % 2 + 1) * 512]
                nc.scalar.activation(buf.rearrange("p (t s) -> p t s", t=TT), x_tok[:, :, k * P:(k + 1) * P],
                                     ACT.Identity, bias=b1[:, k:k + 1], scale=a1[:, k:k + 1]).then_inc(s_h, 1)
                act.wait_ge(s_h, k + 1)
                nc.scalar.activation(h_hi[:, k, :], buf, ACT.Copy).then_inc(s_hhi, 1)

            h_block(0)
            split_hi(1, width=896)
            for k in range(KD - 1):
                split_hi(k + 2, width=896 if k + 2 < KD else SLOT)
                h_block(k + 1)
            split_hi(N_U0 + 1)

            split_hi(N_U0 + 2)
            for t in range(TT):
                act.wait_ge(s_first, t + 1)
                nc.scalar.activation(v_tok[t], ps[t][:, :], ACT.Gelu_apprx_tanh).then_inc(s_vg, 1)
            for i in range(1, HEADS):
                if i < HEADS - 1:
                    act.wait_ge(s_first, TT + i)
                else:
                    act.wait_ge(s_used, KD)
                nc.scalar.activation(u_gelu[i], ps[3 + i][:, :], ACT.Gelu_apprx_tanh).then_inc(s_ug, 1)
            act.wait_ge(s_used, N_U0 + 1)
            nc.scalar.activation(u_gelu[0], ps[7][:, :], ACT.Gelu_apprx_tanh).then_inc(s_ug, 1)

            def xb_copy(g):
                act.wait_ge(s_used, N_XB + g + 1)
                if g >= 1:
                    act.wait_ge(s_p, g)
                nc.scalar.activation(pads[:, 0, PAD:PAD + SEQ], ps[g][:, :], ACT.Copy).then_inc(s_xb, 1)

            def yb_hi(g):
                act.wait_ge(s_pm, g + 1)
                nc.scalar.activation(act_hi[:, YB + g, :], ps[7][:, :], ACT.Copy,
                                     scale=vec[:, V_PSC + g:V_PSC + g + 1]).then_inc(s_ybhi, 1)

            def cg_copy(cc):
                act.wait_ge(s_used, N_CONV + 3 * cc + 1)
                if cc >= 1:
                    act.wait_ge(s_z, cc)
                nc.scalar.activation(cg_sb, ps[3 * cc % 6][:, :], ACT.Copy).then_inc(s_cg, 1)

            def ya_hi(h):
                act.wait_ge(s_ya, h + 1)
                nc.scalar.activation(act_hi[:, YA + h, :], pads[:, 2, PAD:PAD + SEQ], ACT.Copy).then_inc(s_yahi, 1)

            def yc_hi(cc):
                act.wait_ge(s_yc, cc + 1)
                nc.scalar.activation(act_hi[:, YC + cc, :], yc_sb, ACT.Copy).then_inc(s_ychi, 1)

            todo = {0: [(xb_copy, 0)], 1: [(xb_copy, 1)], 2: [(xb_copy, 2), (yb_hi, 0)],
                    3: [(xb_copy, 3), (yb_hi, 1)], 4: [(cg_copy, 0), (ya_hi, 0)], 5: [(yb_hi, 2)],
                    6: [(yc_hi, 0), (ya_hi, 1)], 7: [(cg_copy, 1), (yb_hi, 3)], 8: [(ya_hi, 2)],
                    9: [(yc_hi, 1)], 10: [(cg_copy, 2), (ya_hi, 3)], 12: [(yc_hi, 2)],
                    13: [(cg_copy, 3)], 15: [(yc_hi, 3)]}
            for n in range(N_XB, N_C):
                split_hi(n + AHEAD)
                for step, i in todo.get(n - N_XB, []):
                    step(i)

            def gate_copy(row, pair, j):
                act.wait_ge(s_red, 2 * j + (KD + pair + 1))
                nc.scalar.activation(gate_row[row][:, bass.ds(j * P, P)], ps[4][:, 0:P], ACT.Copy)\
                    .then_inc(s_row, 1)

            with act.Fori(0, KD) as j:
                for b in range(3):
                    n = N_C + b
                    split_hi(n + AHEAD, it=j, width=BIG if b == 1 else SLOT)
                    act.wait_ge(s_used, j * 4 + (n + 1))
                    act.wait_ge(s_ab, j * 2 + KD)
                    nc.scalar.activation(sig[b], ps[b][:, :], ACT.Sigmoid).then_inc(s_sig, 1)
                split_hi(N_C + 3 + AHEAD, it=j)
                act.wait_ge(s_yclo, 4)
                gate_copy(0, 0, j)
                act.wait_ge(s_m, j + 1)
                nc.scalar.activation(act_hi[:, bass.ds(j + MERGED, 1), :], merge[0], ACT.Copy).then_inc(s_mhi, 1)
                gate_copy(1, 1, j)

            for n in range(N_WO + AHEAD, N_UP):
                split_hi(n)

            def square1(t):
                act.wait_ge(s_x1, t + 1)
                if t >= 2:
                    act.wait_ge(s_x1t, 2 * (t - 1))
                nc.scalar.activation(x1n[t % 2], x_tok[:, t, :], ACT.Square,
                                     accum_out=ssq[:, 1, t:t + 1]).then_inc(s_ssq, 1)

            def h2_part(t):
                act.wait_ge(s_x1t, 2 * t + 1)
                if t >= 1:
                    act.wait_ge(s_h2lo, t)
                for k in range(4):
                    last = nc.scalar.activation(h2_tmp[:, k * P:(k + 1) * P], ps[2 * t][:, k * P:(k + 1) * P],
                                                ACT.Identity, bias=cols2[:, 0, k:k + 1], scale=a2[:, k:k + 1])
                last.then_inc(s_h2a, 1)

            def h2_high(t):
                act.wait_ge(s_h2a, t + 1)
                act.wait_ge(s_h2d, t + 1)
                nc.scalar.activation(h_hi[:, :, t * P:(t + 1) * P], h2_tmp.rearrange("p (k s) -> p k s", k=KD),
                                     ACT.Copy).then_inc(s_h2hi, 1)

            square1(0)
            h2_part(0)
            square1(1)
            h2_high(0)
            h2_part(1)
            square1(2)
            split_hi(N_UP)
            h2_high(1)
            split_hi(N_UP + 1)
            square1(3)
            h2_part(2)
            h2_high(2)
            split_hi(N_UP + 2)
            h2_part(3)
            split_hi(N_UP + 3)
            h2_high(3)

            def silu(f, it=None):
                act.wait_ge(s_used, N_UP + 2 * f + 1 if it is None else it * 4 + (N_UP + 2 * f + 1))
                if it is not None:
                    act.wait_ge(s_g, it * 2 + (f - 1))
                nc.scalar.activation(pads[:, f, 0:512], ps[2 * f][:, :], ACT.Silu).then_inc(s_a, 1)

            def hidden_hi(f, it=None):
                act.wait_ge(s_g, f + 1 if it is None else it * 2 + (f + 1))
                at = f if it is None else bass.ds(it * 2 + f, 1)
                nc.scalar.activation(act_hi[:, at, :], tmp[:, f * 512:(f + 1) * 512], ACT.Copy).then_inc(s_ghi, 1)

            silu(0)
            split_hi(N_UP + 4)
            hidden_hi(0)
            split_hi(N_UP + 5)
            silu(1)
            hidden_hi(1)
            with act.Fori(1, KF // 2) as i:
                for f in range(2):
                    n = N_UP + 2 * f
                    split_hi(n + AHEAD, it=i)
                    silu(f, i)
                    split_hi(n + 1 + AHEAD, it=i)
                    hidden_hi(f, i)

            for n in range(N_DOWN + AHEAD, N_END):
                split_hi(n)
            for t in range(TT):
                act.wait_ge(s_x2, t + 1)
                if t >= 1:
                    act.wait_ge(s_ssq, 2 * TT + t)
                nc.scalar.activation(pads[:, 0:2, 0:512], x_tok[:, t, :].rearrange("p (a b) -> p a b", a=2),
                                     ACT.Square, accum_out=ssq[:, 2, t:t + 1]).then_inc(s_ssq, 1)

        @block.vector
        def _(dve):
            part = {"first": 0, "each": 0, "it": None, "steps": 0}

            def link(ins):
                part["steps"] += 1
                ins.then_inc(s_dve, 1)
                n = part["first"] + part["steps"]
                dve.wait_ge(s_dve, n if part["it"] is None else part["it"] * part["each"] + n)

            def split_lo(n, it=None, step=RING, width=SLOT):
                dve.wait_ge(s_whi, n + 1 if it is None else it * step + (n + 1))
                nc.vector.tensor_tensor(lo(n, width), raw(n, width), hi(n, width).bitcast(fp32),
                                        ALU.subtract).then_inc(s_wlo, 1)

            dve.wait_ge(s_vect, 1)
            nc.vector.tensor_copy(vec[:, :], ps[7][:, 0:V_END]).then_inc(s_vecsb, 1)

            def x_copy(t):
                dve.wait_ge(s_xt, 2 * t + 2)
                nc.vector.tensor_copy(x_tok[:, t, 512:1024], ps[2 * (t % 3) + 1][:, :]).then_inc(s_xtd, 1)

            for t in range(TT):
                dve.wait_ge(s_rstd, t + 1)
                nc.vector.tensor_scalar(x_tok[:, t, :], x_tok[:, t, :], rstd[:, 0, t:t + 1], None, ALU.mult)\
                    .then_inc(s_xn, 1)
                if t >= 1:
                    x_copy(t - 1)
            x_copy(3)

            def mod_pair(v, buf, bias, it=None, landed=None):
                dve.wait_ge(s_mod[bias], landed)
                if it is not None or v >= 2:
                    dve.wait_ge(s_red, v - 1 if it is None else it * 2 + (v - 1))
                acc = mod_acc[:, bias, :]
                piece = mod_w[:, buf * 2048:(buf + 1) * 2048].rearrange("p (k n) -> p k n", k=KD)
                link(nc.vector.tensor_scalar(acc, piece[:, 0, :], c_act[:, 0:1], None, ALU.mult))
                for k in range(1, KD):
                    ins = nc.vector.scalar_tensor_tensor(out=acc, in0=piece[:, k, :], scalar=c_act[:, k:k + 1],
                                                         in1=acc, op0=ALU.mult, op1=ALU.add)
                    if k < KD - 1:
                        link(ins)
                ins.then_inc(s_acc, 1)

            def columns1(k):
                dve.wait_ge(s_red, k + 1)
                nc.vector.scalar_tensor_tensor(out=a1[:, k:k + 1], in0=ps[7][:, 0:1], scalar=1.0,
                                               in1=vec[:, V_GMIX + k:V_GMIX + k + 1], op0=ALU.add, op1=ALU.mult)
                nc.vector.tensor_copy(b1[:, k:k + 1], ps[7][:, 1:2]).then_inc(s_ab, 1)

            def h_low(k):
                dve.wait_ge(s_hhi, k + 1)
                nc.vector.tensor_tensor(h_lo[:, k, :], tmp[:, (k % 2) * 512:(k % 2 + 1) * 512],
                                        h_hi[:, k, :].bitcast(fp32), ALU.subtract).then_inc(s_hlo, 1)

            dve.wait_ge(s_c, 1)
            mod_pair(0, 0, 0, landed=64)
            columns1(0)
            split_lo(0, width=896)
            h_low(0)
            split_lo(1, width=896)
            for k in range(KD - 1):
                v = k + 1
                mod_pair(v, v % 2, v % 2, landed=64 * (v // 2 + 1))
                columns1(k + 1)
                split_lo(k + 2, width=896 if k + 2 < KD else SLOT)
                h_low(k + 1)
            split_lo(N_U0 + 1)

            split_lo(N_U0 + 2)
            for t in range(TT):
                dve.wait_ge(s_vg, t + 1)
                link(nc.vector.bn_stats(stats[:, t, :], v_tok[t]))
                nc.vector.bn_aggr(mv[:, t, :], stats[:, t, :]).then_inc(s_mv, 1)

            def v_norm():
                dve.wait_ge(s_lnr, 1)
                for t in range(TT):
                    nc.vector.tensor_scalar(v_tok[t], v_tok[t], mv[:, t, 0:1], rstd[:, 1, t:t + 1],
                                            ALU.subtract, ALU.mult).then_inc(s_vn, 1)

            def pool(g):
                win = WINDOWS[g]
                dve.wait_ge(s_xb, g + 1)
                src = 0
                for lev in range(g + 1):
                    lag = 1 << lev
                    dst = 1 + lev % 2
                    link(nc.vector.tensor_tensor(pads[:, dst, PAD:PAD + SEQ], pads[:, src, PAD:PAD + SEQ],
                                                 pads[:, src, PAD - lag:PAD + SEQ - lag], ALU.add))
                    src = dst
                if g >= 2:
                    dve.wait_ge(s_pm, g - 1)
                p = tmp[:, (g % 2) * 512:(g % 2 + 1) * 512]
                link(nc.vector.tensor_tensor(fix[:, 0:win - 1], pads[:, src, PAD:PAD + win - 1],
                                             recip[:, 0:win - 1], ALU.mult))
                nc.vector.scalar_tensor_tensor(out=p[:, win - 1:SEQ], in0=pads[:, src, PAD + win - 1:PAD + SEQ],
                                               scalar=1.0 / win, in1=pads[:, 0, PAD + win - 1:PAD + SEQ],
                                               op0=ALU.mult, op1=ALU.subtract)
                nc.vector.tensor_tensor(p[:, 0:win - 1], fix[:, 0:win - 1], pads[:, 0, PAD:PAD + win - 1],
                                        ALU.subtract).then_inc(s_p, 1)

            def ws_copy():
                dve.wait_ge(s_wst, 1)
                nc.vector.tensor_copy(ws_t, ps[6][:, :]).then_inc(s_wsc, 1)

            def bias_rows():
                dve.wait_ge(s_rs, 1)
                for h in range(HEADS):
                    last = nc.vector.scalar_tensor_tensor(
                        out=gate_bias[:, h * P:(h + 1) * P], in0=ps[6][:, h * P:(h + 1) * P],
                        scalar=vec[:, V_LNB + h:V_LNB + h + 1], in1=bs_row[:, h * P:(h + 1) * P],
                        op0=ALU.mult, op1=ALU.add)
                last.then_inc(s_gb, 1)

            def yb_low(g):
                dve.wait_ge(s_ybhi, g + 1)
                nc.vector.scalar_tensor_tensor(out=act_lo[:, YB + g, :], in0=ps[7][:, :],
                                               scalar=vec[:, V_PSC + g:V_PSC + g + 1],
                                               in1=act_hi[:, YB + g, :].bitcast(fp32),
                                               op0=ALU.mult, op1=ALU.subtract).then_inc(s_yblo, 1)

            def gating(h):
                dve.wait_ge(s_gm, h + 1)
                dve.wait_ge(s_p, 4)
                s = pads[:, 2, PAD:PAD + SEQ]
                bias = gate_bias[:, h * P:(h + 1) * P].rearrange("p (o t) -> p o t", o=1).broadcast_to((P, TT, P))
                nc.vector.scalar_tensor_tensor(out=s.rearrange("p (n t) -> p n t", n=TT),
                                               in0=ps[6][:, :].rearrange("p (n t) -> p n t", n=TT),
                                               scalar=vec[:, V_LNG + h:V_LNG + h + 1], in1=bias,
                                               op0=ALU.mult, op1=ALU.add).then_inc(s_gmr, 1)
                dve.wait_ge(s_gmr, h + 1)
                dve.wait_ge(s_ug, 4)
                nc.vector.tensor_tensor(s, s, u_gelu[h], ALU.mult).then_inc(s_ya, 1)
                dve.wait_ge(s_yahi, h + 1)
                nc.vector.tensor_tensor(act_lo[:, YA + h, :], s, act_hi[:, YA + h, :].bitcast(fp32),
                                        ALU.subtract)

            def conv(cc):
                z = pads[:, cc % 2, :]
                dve.wait_ge(s_used, N_CONV + 3 * cc + 2)
                dve.wait_ge(s_cg, cc + 1)
                dve.wait_ge(s_p, 4)
                nc.vector.tensor_tensor(z[:, PAD:PAD + SEQ], ps[(3 * cc + 1) % 6][:, :], cg_sb, ALU.mult)\
                    .then_inc(s_z, 1)
                dve.wait_ge(s_z, cc + 1)
                w = [vec[:, V_CONV + 4 * i + cc:V_CONV + 4 * i + cc + 1] for i in range(3)]
                link(nc.vector.tensor_scalar(taps, z[:, PAD - 2:PAD - 2 + SEQ], w[0], None, ALU.mult))
                for i in (1, 2):
                    link(nc.vector.scalar_tensor_tensor(out=taps, in0=z[:, PAD - 2 + i:PAD - 2 + i + SEQ],
                                                        scalar=w[i], in1=taps, op0=ALU.mult, op1=ALU.add))

            def conv_gate(cc):
                dve.wait_ge(s_used, N_CONV + 3 * cc + 3)
                nc.vector.tensor_tensor(yc_sb, ps[(3 * cc + 2) % 6][:, :], taps, ALU.mult).then_inc(s_yc, 1)
                dve.wait_ge(s_ychi, cc + 1)
                nc.vector.tensor_tensor(act_lo[:, YC + cc, :], yc_sb, act_hi[:, YC + cc, :].bitcast(fp32),
                                        ALU.subtract).then_inc(s_yclo, 1)

            todo = {0: [(v_norm,), (pool, 0)], 1: [(pool, 1), (ws_copy,)], 2: [(pool, 2), (bias_rows,), (yb_low, 0)],
                    3: [(pool, 3), (yb_low, 1)], 4: [(gating, 0)], 5: [(conv, 0), (yb_low, 2)],
                    6: [(conv_gate, 0), (gating, 1)], 7: [(yb_low, 3)], 8: [(conv, 1), (gating, 2)],
                    9: [(conv_gate, 1)], 10: [(gating, 3)], 11: [(conv, 2)], 12: [(conv_gate, 2)],
                    14: [(conv, 3)], 15: [(conv_gate, 3)]}
            for n in range(N_XB, N_C):
                split_lo(n + AHEAD)
                for step, *i in todo.get(n - N_XB, []):
                    step(*i)

            part["first"] += part["steps"]
            links = 2 * (KD - 1) + 1
            with dve.Fori(0, KD) as j:
                part.update(it=j, each=links, steps=0)
                split_lo(N_C + AHEAD, it=j)
                mod_pair(KD, 0, 0, it=j, landed=j * 64 + 64 * (KD // 2 + 1))
                split_lo(N_C + 1 + AHEAD, it=j, width=BIG)
                split_lo(N_C + 2 + AHEAD, it=j)
                mod_pair(KD + 1, 0, 1, it=j, landed=j * 64 + 64 * (KD // 2 + 1))
                split_lo(N_C + 3 + AHEAD, it=j)
                dve.wait_ge(s_red, j * 2 + (KD + 1))
                nc.vector.tensor_copy(cols2[:, 0, bass.ds(j, 1)], ps[3][:, 0:1]).then_inc(s_ab, 1)
                dve.wait_ge(s_sig, j * 3 + 3)
                for b in range(3):
                    if b < 2:
                        dve.wait_ge(s_yp, j * 2 + (b + 1))
                    else:
                        dve.wait_ge(s_used, j * 4 + (N_C + 4))
                    nc.vector.tensor_tensor(merge[min(b, 1)], ps[5 + b][:, :], sig[b], ALU.mult).then_inc(s_y, 1)
                    dve.wait_ge(s_y, j * 3 + (b + 1))
                    if b == 1:
                        link(nc.vector.tensor_tensor(merge[0], merge[0], merge[1], ALU.add))
                    if b == 2:
                        nc.vector.tensor_tensor(merge[0], merge[0], merge[1], ALU.add).then_inc(s_m, 1)
                dve.wait_ge(s_mhi, j + 1)
                nc.vector.tensor_tensor(act_lo[:, bass.ds(j + MERGED, 1), :], merge[0],
                                        act_hi[:, bass.ds(j + MERGED, 1), :].bitcast(fp32),
                                        ALU.subtract).then_inc(s_mlo, 1)
                dve.wait_ge(s_red, j * 2 + (KD + 2))
                nc.vector.tensor_copy(cols2[:, 1, bass.ds(j, 1)], ps[3][:, 0:1]).then_inc(s_ab, 1)
            assert part["steps"] == links
            part.update(it=None, first=part["first"] + KD * links, steps=0)

            dve.wait_ge(s_ab, 3 * KD)
            link(nc.vector.scalar_tensor_tensor(out=a2[:, :], in0=cols2[:, 1, :], scalar=1.0,
                                                in1=vec[:, V_GFFN:V_GFFN + KD], op0=ALU.add, op1=ALU.mult))
            for n in range(N_WO + AHEAD, N_UP):
                split_lo(n)

            def residual(t, done, used, row, ready):
                if t < TT - 1:
                    dve.wait_ge(done, t + 1)
                else:
                    dve.wait_ge(s_used, used)
                if t >= 1:
                    dve.wait_ge(ready, t)
                for q in range(2):
                    ins = nc.vector.tensor_tensor(tmp[:, q * 512:(q + 1) * 512], ps[2 * t + q][:, :],
                                                  row[:, q * 512:(q + 1) * 512], ALU.mult)
                link(ins)
                nc.vector.tensor_tensor(x_tok[:, t, :], x_tok[:, t, :], tmp[:, :], ALU.add).then_inc(ready, 1)

            def x1_tile(t):
                if t == 0:
                    dve.wait_ge(s_row, 2 * KD)
                dve.wait_ge(s_x[t], 32)
                residual(t, s_wo, N_UP, gate_row[0], s_x1)

            def x1_norm(t):
                dve.wait_ge(s_rstd, TT + t + 1)
                nc.vector.tensor_scalar(x1n[t % 2], x_tok[:, t, :], rstd[:, 2, t:t + 1], None, ALU.mult)\
                    .then_inc(s_x1n, 1)

            def h2_part(t):
                dve.wait_ge(s_x1t, 2 * t + 2)
                if t >= 1:
                    dve.wait_ge(s_h2lo, t)
                for k in range(4, KD):
                    last = nc.vector.tensor_scalar(h2_tmp[:, k * P:(k + 1) * P],
                                                   ps[2 * t + 1][:, (k - 4) * P:(k - 3) * P],
                                                   a2[:, k:k + 1], cols2[:, 0, k:k + 1], ALU.mult, ALU.add)
                last.then_inc(s_h2d, 1)

            def h2_low(t):
                dve.wait_ge(s_h2hi, t + 1)
                nc.vector.tensor_tensor(h_lo[:, :, t * P:(t + 1) * P], h2_tmp.rearrange("p (k s) -> p k s", k=KD),
                                        h_hi[:, :, t * P:(t + 1) * P].bitcast(fp32), ALU.subtract)\
                    .then_inc(s_h2lo, 1)

            x1_tile(0)
            x1_norm(0)
            x1_tile(1)
            h2_part(0)
            x1_norm(1)
            h2_low(0)
            x1_tile(2)
            h2_part(1)
            split_lo(N_UP)
            x1_norm(2)
            h2_low(1)
            x1_tile(3)
            split_lo(N_UP + 1)
            h2_part(2)
            x1_norm(3)
            h2_low(2)
            split_lo(N_UP + 2)
            h2_part(3)
            split_lo(N_UP + 3)
            h2_low(3)

            def hidden(f, it=None):
                dve.wait_ge(s_used, N_UP + 2 * f + 2 if it is None else it * 4 + (N_UP + 2 * f + 2))
                dve.wait_ge(s_a, f + 1 if it is None else it * 2 + (f + 1))
                nc.vector.tensor_tensor(tmp[:, f * 512:(f + 1) * 512], ps[2 * f + 1][:, :], pads[:, f, 0:512],
                                        ALU.mult).then_inc(s_g, 1)

            def hidden_low(f, it=None):
                dve.wait_ge(s_ghi, f + 1 if it is None else it * 2 + (f + 1))
                at = slice(f, f + 1) if it is None else bass.ds(it * 2 + f, 1)
                nc.vector.tensor_tensor(act_lo[:, at, :], tmp[:, f * 512:(f + 1) * 512],
                                        act_hi[:, at, :].bitcast(fp32), ALU.subtract).then_inc(s_glo, 1)

            split_lo(N_UP + 4)
            hidden(0)
            hidden_low(0)
            split_lo(N_UP + 5)
            hidden(1)
            hidden_low(1)
            with dve.Fori(1, KF // 2) as i:
                for f in range(2):
                    n = N_UP + 2 * f
                    split_lo(n + AHEAD, it=i)
                    split_lo(n + 1 + AHEAD, it=i)
                    hidden(f, i)
                    hidden_low(f, i)

            for n in range(N_DOWN + AHEAD, N_END):
                split_lo(n)
            dve.wait_ge(s_gfin, 16)

            def out_tile(t):
                dve.wait_ge(s_rstd, 2 * TT + t + 1)
                for q in range(2):
                    part_x = x_tok[:, t, q * 512:(q + 1) * 512]
                    nc.vector.scalar_tensor_tensor(out=part_x, in0=part_x, scalar=rstd[:, 3, t:t + 1],
                                                   in1=gfin_row[:, q * 512:(q + 1) * 512],
                                                   op0=ALU.mult, op1=ALU.mult).then_inc(s_o, 1)

            for t in range(TT):
                residual(t, s_dn, N_END, gate_row[1], s_x2)
                if t >= 1:
                    out_tile(t - 1)
            out_tile(TT - 1)

        @block.tensor
        def _(pe):
            def three(dst, w, m, start, stop):
                nc.tensor.matmul(dst, w[0], m[0], start=start, stop=False)
                nc.tensor.matmul(dst, w[1], m[0], start=False, stop=False)
                return nc.tensor.matmul(dst, w[0], m[1], start=False, stop=stop)

            def weights(n, a, width=P):
                return hi(n, BIG if n % RING == 0 else SLOT)[:, a:a + width], \
                    lo(n, BIG if n % RING == 0 else SLOT)[:, a:a + width]

            def slab_ready(n, it=None, step=RING):
                pe.wait_ge(s_whi, n + 1 if it is None else it * step + (n + 1))
                pe.wait_ge(s_wlo, n + 1 if it is None else it * step + (n + 1))

            def hT(k, a=0, b=SEQ):
                return h_hi[:, k, a:b], h_lo[:, k, a:b]

            def acts(k, a=0, b=SEQ):
                return act_hi[:, k, a:b], act_lo[:, k, a:b]

            def project(n, bank, it=None, a=0, b=SEQ, used=True):
                slab_ready(n, it)
                for k in range(KD):
                    last = three(ps[bank][:, a:b], weights(n, k * P), hT(k, a, b), k == 0, k == KD - 1)
                if used:
                    last.then_inc(s_used, 1)

            pe.wait_ge(s_const, 2)
            pe.wait_ge(s_vec, 7 * 16)
            nc.tensor.transpose(ps[7][:, 0:V_END], rows[0:V_END, :], ident[0:V_END, 0:V_END]).then_inc(s_vect, 1)
            for t in range(TT):
                pe.wait_ge(s_xn, t + 1)
                if t == 3:
                    pe.wait_ge(s_xta, 1)
                    pe.wait_ge(s_xtd, 1)
                for q in range(2):
                    for i in range(4):
                        k = 4 * q + i
                        last = nc.tensor.transpose(ps[2 * (t % 3) + q][:, i * P:(i + 1) * P],
                                                   x_tok[:, t, k * P:(k + 1) * P], ident[:, :])
                    last.then_inc(s_xt, 1)

            def column(dst, bias, m):
                nc.tensor.matmul(dst, mod_acc[:, bias, m * P:(m + 1) * P], ones[:, 0:1], start=True, stop=False)
                return nc.tensor.matmul(dst, mod_b[:, bias, m * P:(m + 1) * P], ones[:, 0:1],
                                        start=False, stop=True)

            def row(dst, bias, m):
                nc.tensor.matmul(dst, ones[:, :], mod_acc[:, bias, m * P:(m + 1) * P], start=True, stop=False)
                return nc.tensor.matmul(dst, ones[:, :], mod_b[:, bias, m * P:(m + 1) * P],
                                        start=False, stop=True)

            def reduce1(k):
                pe.wait_ge(s_acc, k + 1)
                if k == 0:
                    pe.wait_ge(s_vecsb, 1)
                else:
                    pe.wait_ge(s_ab, k)
                column(ps[7][:, 0:1], k % 2, 0)
                column(ps[7][:, 1:2], k % 2, 1).then_inc(s_red, 1)

            reduce1(0)
            pe.wait_ge(s_xta, TT)
            pe.wait_ge(s_xtd, TT)
            V0 = COL_V - P

            def product(k, i):
                if i < TT:
                    return (h_hi[:, k, i * P:(i + 1) * P], h_lo[:, k, i * P:(i + 1) * P]), \
                        weights(k, V0, 512)
                return weights(k, (i - 4) * P), hT(k)

            for k in range(KD):
                pe.wait_ge(s_whi, k + 1)
                pe.wait_ge(s_hhi, k + 1)
                if k < KD - 1:
                    for i in range(7):
                        w, m = product(k, i)
                        nc.tensor.matmul(ps[i][:, :], w[0], m[0], start=k == 0, stop=False)
                    reduce1(k + 1)
                    pe.wait_ge(s_wlo, k + 1)
                    for i in range(7):
                        w, m = product(k, i)
                        nc.tensor.matmul(ps[i][:, :], w[1] if i >= TT else w[0], m[0] if i >= TT else m[1],
                                         start=False, stop=False)
                    pe.wait_ge(s_hlo, k + 1)
                    for i in range(7):
                        w, m = product(k, i)
                        last = nc.tensor.matmul(ps[i][:, :], w[0] if i >= TT else w[1],
                                                m[1] if i >= TT else m[0], start=False, stop=False)
                    last.then_inc(s_used, 1)
                else:
                    pe.wait_ge(s_wlo, k + 1)
                    pe.wait_ge(s_hlo, k + 1)
                    for i in range(7):
                        three(ps[i][:, :], *product(k, i), False, True).then_inc(s_first if i < 6 else s_used, 1)

            def ws_transpose():
                pe.wait_ge(s_mask, 1)
                pe.wait_ge(s_ug, 3)
                for h in range(HEADS):
                    last = nc.tensor.transpose(ps[6][:, h * P:(h + 1) * P], ws_raw[:, h * P:(h + 1) * P],
                                               ident[:, :])
                last.then_inc(s_wst, 1)

            def ws_rowsum():
                pe.wait_ge(s_wsc, 1)
                nc.tensor.matmul(ps[6][:, :], ones[:, :], ws_t, start=True, stop=True).then_inc(s_rs, 1)

            def pool_map(g):
                pe.wait_ge(s_p, g + 1)
                if g == 0:
                    pe.wait_ge(s_ug, 4)
                else:
                    pe.wait_ge(s_yblo, g)
                nc.tensor.matmul(ps[7][:, :], pool_sb[:, g * P:(g + 1) * P], tmp[:, (g % 2) * 512:(g % 2 + 1) * 512],
                                 start=True, stop=True).then_inc(s_pm, 1)

            def gate_tokens(h):
                if h == 0:
                    pe.wait_ge(s_gb, 1)
                    pe.wait_ge(s_vn, TT)
                else:
                    pe.wait_ge(s_gmr, h)
                for t in range(TT):
                    last = nc.tensor.matmul(ps[6][:, t * P:(t + 1) * P], v_tok[t][:, h * P:(h + 1) * P],
                                            ws_t[:, h * P:(h + 1) * P], start=True, stop=True)
                last.then_inc(s_gm, 1)

            pe.wait_ge(s_ab, KD)
            project(N_U0, 7)
            todo = {1: [(ws_transpose,)], 2: [(ws_rowsum,), (pool_map, 0)], 3: [(pool_map, 1)],
                    4: [(gate_tokens, 0)], 5: [(pool_map, 2)], 6: [(gate_tokens, 1)],
                    7: [(pool_map, 3)], 8: [(gate_tokens, 2)], 10: [(gate_tokens, 3)]}
            for n in range(N_XB, N_C):
                if n < N_CONV:
                    bank = n - N_XB
                    pe.wait_ge(s_vg, bank + 1)
                else:
                    m = n - N_CONV
                    bank = m % 6
                    if m < 4:
                        pe.wait_ge(s_xb, m + 1)
                    elif m >= 6:
                        pe.wait_ge((s_cg, s_z, s_yc)[m % 3], m // 3 - 1)
                project(n, bank)
                for step, *i in todo.get(n - N_XB, []):
                    step(*i)

            pe.wait_ge(s_cg, 3)
            pe.wait_ge(s_z, 3)
            pe.wait_ge(s_yc, 3)
            with pe.Fori(0, KD) as j:
                for b in range(3):
                    project(N_C + b, b, it=j)
                pe.wait_ge(s_acc, j * 2 + (KD + 1))
                pe.wait_ge(s_ab, j * 2 + KD)
                pe.wait_ge(s_yc, 4)
                column(ps[3][:, 0:1], 0, 1)
                row(ps[4][:, 0:P], 0, 0).then_inc(s_red, 1)
                slab_ready(N_C + 3, it=j)
                pe.wait_ge(s_yblo, 4)
                pe.wait_ge(s_yclo, 4)
                for b, first in enumerate((YA, YB, YC)):
                    for k in range(KW):
                        last = three(ps[5 + b][:, :], weights(N_C + 3, (b * KW + k) * P), acts(first + k),
                                     k == 0, k == KW - 1)
                    last.then_inc(s_yp if b < 2 else s_used, 1)
                pe.wait_ge(s_acc, j * 2 + (KD + 2))
                pe.wait_ge(s_ab, j * 2 + (KD + 1))
                pe.wait_ge(s_row, j * 2 + 1)
                column(ps[3][:, 0:1], 1, 0)
                row(ps[4][:, 0:P], 1, 1).then_inc(s_red, 1)

            def token_product(n, k, t, first, last):
                for q in range(2):
                    ins = three(ps[2 * t + q][:, :], acts(k, t * P, (t + 1) * P), weights(n, q * 512, 512),
                                first, last)
                return ins

            for k in range(4):
                slab_ready(N_WO + k)
                pe.wait_ge(s_mlo, k + 1)
                for t in range(TT):
                    if k == 0 and t == 0:
                        pe.wait_ge(s_sig, 3 * KD)
                    if k == 0 and t == 1:
                        pe.wait_ge(s_ab, 3 * KD)
                        pe.wait_ge(s_row, 2 * KD)
                    if k == 0 and t == 2:
                        pe.wait_ge(s_y, 3 * KD - 2)
                    if k == 0 and t == 3:
                        pe.wait_ge(s_y, 3 * KD)
                    last = token_product(N_WO + k, MERGED + k, t, k == 0, False)
                last.then_inc(s_used, 1)

            def x1_transpose(t):
                pe.wait_ge(s_x1n, t + 1)
                for q in range(2):
                    for i in range(4):
                        k = 4 * q + i
                        last = nc.tensor.transpose(ps[2 * t + q][:, i * P:(i + 1) * P],
                                                   x1n[t % 2][:, k * P:(k + 1) * P], ident[:, :])
                    last.then_inc(s_x1t, 1)

            for t in range(TT):
                for k in range(4, KD):
                    if t == 0:
                        slab_ready(N_WO + k)
                        pe.wait_ge(s_mlo, k + 1)
                    last = token_product(N_WO + k, MERGED + k, t, False, k == KD - 1)
                    if t == TT - 1:
                        last.then_inc(s_used, 1)
                if t < TT - 1:
                    last.then_inc(s_wo, 1)
                if t >= 1:
                    x1_transpose(t - 1)

            for m in range(2):
                pe.wait_ge(s_h2a, 2)
                pe.wait_ge(s_h2lo, 2)
                for i in range(2):
                    project(N_UP + 2 * m + i, 2 * m + i, a=0, b=2 * P, used=False)
                if m == 0:
                    x1_transpose(TT - 1)
            pe.wait_ge(s_h2lo, TT)
            for i in range(4):
                project(N_UP + i, i, a=2 * P, b=SEQ)
            with pe.Fori(1, KF // 2) as i:
                for f in range(2):
                    pe.wait_ge(s_a, i * 2 + (f - 1))
                    project(N_UP + 2 * f, 2 * f, it=i)
                    pe.wait_ge(s_g, i * 2 + (f - 1))
                    project(N_UP + 2 * f + 1, 2 * f + 1, it=i)

            for k in range(KF - 4):
                slab_ready(N_DOWN + k)
                for t in (2, 3, 0, 1):
                    if k == 0 and t == 0:
                        pe.wait_ge(s_a, KF)
                        pe.wait_ge(s_g, KF)
                    pe.wait_ge(s_glo, k + 1)
                    last = token_product(N_DOWN + k, k, t, k == 0, False)
                last.then_inc(s_used, 1)
            for t in range(TT):
                for k in range(KF - 4, KF):
                    if t == 0:
                        slab_ready(N_DOWN + k)
                        pe.wait_ge(s_glo, k + 1)
                    last = token_product(N_DOWN + k, k, t, False, k == KF - 1)
                    if t == TT - 1:
                        last.then_inc(s_used, 1)
                if t < TT - 1:
                    last.then_inc(s_dn, 1)


_INS = ["x", "c", "w_mod", "b_mod", "g_mix", "w_in", "gm_ln_g", "gm_ln_b", "gm_w_s", "gm_b_s", "w_pa",
        "pool_w", "pool_scale", "w_pb", "conv_w", "w_pc", "w_o", "g_ffn", "w_13", "w_2", "g_final"]
_SQUEEZE = {"x", "w_mod", "w_in", "gm_w_s", "gm_b_s", "w_pa", "pool_w", "w_pb", "conv_w", "w_pc", "w_o",
            "w_13", "w_2"}


def kernel(**inputs):
    import numpy as np
    import concourse.bacc as bacc
    from concourse.bass_utils import run_bass_kernel_spmd

    nc = bacc.Bacc("TRN2", target_bir_lowering=False, num_devices=1, dynamic_dma_scratch_size=1024)
    arrays, args = {}, []
    for name in _INS:
        a = np.ascontiguousarray(inputs[name])
        if name in _SQUEEZE:
            a = a.reshape(a.shape[1:])
        arrays[f"in_{name}"] = a
        args.append(nc.dram_tensor(f"in_{name}", a.shape, mybir.dt.from_np(a.dtype), kind="ExternalInput").ap())
    out = nc.dram_tensor("out", (SEQ, D), fp32, kind="ExternalOutput").ap()
    build(nc, *args, out)
    r = run_bass_kernel_spmd(nc, [arrays], core_ids=[0])
    return r.results[0]["out"].reshape(1, SEQ, D)
```

```python
import concourse.bass as bass
from concourse import mybir
from contextlib import ExitStack

fp32 = mybir.dt.float32
fp32r = mybir.dt.float32r
ALU = mybir.AluOpType
ACT = mybir.ActivationFunctionType

P = 128
D = 1024
SEQ = 512
TT = SEQ // P
KD = D // P
HEADS = 4
WIDTH = 512
KW = WIDTH // P
WINDOWS = (2, 4, 8, 16)
DFF = 2816
KF = DFF // P
EPS = 1e-6
RING = 4
SLOT = 1024
BIG = 3 * KW * P
PAD = 16

COL_U, COL_V, COL_XB, COL_BG, COL_CG, COL_HC, COL_GATE = 0, 512, 1024, 1536, 2048, 2560, 3072

N_A = 0
N_U0 = N_A + KD
N_XB = N_U0 + 1
N_CONV = N_XB + 4
N_C = N_CONV + 12
N_WO = N_C + 4 * KD
N_UP = N_WO + KD
N_DOWN = N_UP + 2 * KF
N_END = N_DOWN + KF
AHEAD = 2

V_C, V_GMIX, V_GFFN, V_PSC, V_CONV, V_LNG, V_LNB, V_END = 0, 8, 16, 24, 28, 40, 44, 48

YA, YB, YC, MERGED = 0, 4, 8, 12


def slot_at(n):
    s = n % RING
    return 0 if s == 0 else BIG + SLOT * (s - 1)


def build(nc, x, c, w_mod, b_mod, g_mix, w_in, gm_ln_g, gm_ln_b, gm_w_s, gm_b_s, w_pa, pool_w,
          pool_scale, w_pb, conv_w, w_pc, w_o, g_ffn, w_13, w_2, g_final, out):
    ctx = ExitStack()
    with ctx:
        def sb(name, shape, dt=fp32):
            return ctx.enter_context(nc.sbuf_tensor(name, shape, dt))

        def sem(name):
            return ctx.enter_context(nc.semaphore(name))

        x_tok = sb("x_tok", [P, TT, D])
        raw_w = sb("raw_w", [P, BIG + 3 * SLOT])
        w_hi = sb("w_hi", [P, BIG + 3 * SLOT], fp32r)
        w_lo = sb("w_lo", [P, BIG + 3 * SLOT], fp32r)
        h_hi = sb("h_hi", [P, KD, SEQ], fp32r)
        h_lo = sb("h_lo", [P, KD, SEQ], fp32r)
        act_hi = sb("act_hi", [P, KF, SEQ], fp32r)
        act_lo = sb("act_lo", [P, KF, SEQ], fp32r)
        mod_w = sb("mod_w", [P, 4 * 1024])
        mod_b = sb("mod_b", [P, 2, 256])
        mod_acc = sb("mod_acc", [P, 2, 256])
        pads = sb("pads", [P, 3, PAD + SEQ])
        tmp = sb("tmp", [P, D])
        ident = sb("ident", [P, P])
        ones = sb("ones", [P, P])
        rows = sb("rows", [P, P])
        vec = sb("vec", [P, V_END])
        c_act = sb("c_act", [P, KD])
        a1 = sb("a1", [P, KD])
        b1 = sb("b1", [P, KD])
        cols2 = sb("cols2", [P, 2, KD])
        a2 = sb("a2", [P, KD])
        recip = sb("recip", [P, PAD])
        half = sb("half", [P, TT])
        ssq = sb("ssq", [P, 3, TT])
        ssq_last = sb("ssq_last", [P, 6])
        ms = sb("ms", [P, 4, TT])
        rstd = sb("rstd", [P, 4, TT])
        stats = sb("stats", [P, TT, 6])
        mv = sb("mv", [P, TT, 2])
        fix = sb("fix", [P, PAD])

        ws_raw = mod_w[:, 0:512]
        ws_t = mod_w[:, 512:1024]
        bs_row = mod_w[:, 1024:1536]
        gate_bias = mod_w[:, 1536:2048]
        pool_sb = mod_w[:, 2048:2560]
        cg_sb = mod_w[:, 2560:3072]
        taps = mod_w[:, 3072:3584]
        yc_sb = mod_w[:, 3584:4096]
        gate_row = [mod_w[:, 2048:3072], mod_w[:, 3072:4096]]
        h2_tmp = mod_w[:, 0:1024]
        gfin_row = mod_w[:, 1024:2048]
        x1n = [mod_w[:, 1024:2048], pads[:, :, :].rearrange("p a b -> p (a b)")[:, 0:D]]
        c_rows = pads[0:KD, 1, PAD:PAD + P]
        flat_x = x_tok[:, :, :].rearrange("p t d -> p (t d)")
        v_tok = [flat_x[:, i * 512:(i + 1) * 512] for i in range(4)]
        u_gelu = [flat_x[:, 2048 + i * 512:2048 + (i + 1) * 512] for i in range(4)]
        sig = [flat_x[:, i * 512:(i + 1) * 512] for i in range(3)]
        merge = [flat_x[:, 1536 + i * 512:1536 + (i + 1) * 512] for i in range(2)]

        ps = [ctx.enter_context(nc.psum_tensor(f"bank{i}", [P, 512], fp32)) for i in range(8)]

        s_x = [sem(f"x_landed{t}") for t in range(TT)]
        s_vec = sem("vectors_landed")
        s_cl = sem("c_landed")
        s_small = sem("branch_weights_landed")
        s_gfin = sem("gfinal_landed")
        s_raw = [sem(f"raw_landed{i}") for i in range(RING)]
        s_mod = [sem(f"mod_landed{i}") for i in range(2)]
        s_mod2 = [sem(f"mod_second_half_landed{i}") for i in range(2)]
        s_out = sem("out_stored")
        s_const = sem("constants_ready")
        s_zero = sem("zeros_ready")
        s_whi = sem("slab_hi_ready")
        s_wlo = sem("slab_lo_ready")
        s_used = sem("slab_used")
        s_vect = sem("vectors_transposed")
        s_vecsb = sem("vectors_in_sbuf")
        s_c = sem("c_act_ready")
        s_ssq = sem("squares_summed")
        s_ms = sem("mean_squares_ready")
        s_rstd = sem("rstd_ready")
        s_xn = sem("x_normed")
        s_xt = sem("x_transposed")
        s_xta = sem("x_transposed_copied_act")
        s_xtd = sem("x_transposed_copied_dve")
        s_acc = sem("mod_accumulated")
        s_red = sem("mod_reduced")
        s_ab = sem("mod_columns_read")
        s_row = sem("mod_gate_row_copied")
        s_h = sem("h_fp32_ready")
        s_hhi = sem("h_hi_ready")
        s_hlo = sem("h_lo_ready")
        s_vg = sem("v_gelu_ready")
        s_ug = sem("u_gelu_ready")
        s_mv = sem("ln_stats_ready")
        s_lnr = sem("ln_rstd_ready")
        s_vn = sem("v_normed")
        s_mask = sem("ws_masked")
        s_wst = sem("ws_transposed")
        s_wsc = sem("ws_transposed_copied")
        s_rs = sem("ws_rowsums_ready")
        s_gb = sem("gate_bias_ready")
        s_first = sem("first_stage_tile_ready")
        s_gm = sem("gating_matmuls_done")
        s_gmr = sem("gating_read")
        s_ya = sem("y_a_ready")
        s_yahi = sem("y_a_hi_ready")
        s_xb = sem("xb_copied")
        s_p = sem("pooled_ready")
        s_pm = sem("pool_map_ready")
        s_ybhi = sem("y_b_hi_ready")
        s_yblo = sem("y_b_lo_ready")
        s_cg = sem("cg_copied")
        s_z = sem("hc_read")
        s_yc = sem("y_c_ready")
        s_ychi = sem("y_c_hi_ready")
        s_yclo = sem("y_c_lo_ready")
        s_sig = sem("gate_sigmoid_ready")
        s_y = sem("branch_products_read")
        s_m = sem("merged_ready")
        s_mhi = sem("merged_hi_ready")
        s_mlo = sem("merged_lo_ready")
        s_wo = sem("mixed_ready")
        s_x1 = sem("x1_ready")
        s_x1n = sem("x1_normed")
        s_x1t = sem("x1_transposed")
        s_h2a = sem("h2_read_act")
        s_h2d = sem("h2_read_dve")
        s_h2hi = sem("h2_hi_ready")
        s_h2lo = sem("h2_lo_ready")
        s_a = sem("silu_ready")
        s_g = sem("hidden_ready")
        s_ghi = sem("hidden_hi_ready")
        s_glo = sem("hidden_lo_ready")
        s_yp = sem("branch_projected")
        s_dn = sem("ffn_out_ready")
        s_x2 = sem("x2_ready")
        s_xg = sem("x2_times_g_ready")
        s_o = sem("out_ready")
        s_ol = sem("last_half_ready")
        s_dve = sem("vector_step")

        w_in_k = w_in.rearrange("(k p) n -> p k n", p=P)
        w_mod_k = w_mod.rearrange("(k p) (m n) -> p k m n", p=P, m=6)
        b_mod_m = b_mod.rearrange("o (m n) -> o m n", m=6)
        w_13_k = w_13.rearrange("(k p) n -> p k n", p=P)
        w_p_k = [w.rearrange("(k p) n -> p k n", p=P) for w in (w_pa, w_pb, w_pc)]

        def raw(n, width=SLOT):
            return raw_w[:, slot_at(n):slot_at(n) + width]

        def hi(n, width=SLOT):
            return w_hi[:, slot_at(n):slot_at(n) + width]

        def lo(n, width=SLOT):
            return w_lo[:, slot_at(n):slot_at(n) + width]

        def mod_slot(i):
            return mod_w[:, i * 2048:(i + 1) * 2048].rearrange("p (k m n) -> p k m n", k=KD, m=2)

        def slab_low(engine, n, width=SLOT):
            engine.tensor_tensor(lo(n, width), raw(n, width), hi(n, width).bitcast(fp32),
                                 ALU.subtract).then_inc(s_wlo, 1)

        def tile_low(engine, t):
            engine.tensor_tensor(h_lo[:, :, t * P:(t + 1) * P], h2_tmp.rearrange("p (k s) -> p k s", k=KD),
                                 h_hi[:, :, t * P:(t + 1) * P].bitcast(fp32), ALU.subtract).then_inc(s_h2lo, 1)

        block = ctx.enter_context(nc.Block())

        @block.sync
        def _(sp):
            def early(*values):
                for v in values:
                    sp.compute_val(v)

            def load(n, dst, src, it=None, step=RING):
                if n >= RING:
                    sp.wait_ge(s_wlo, n - 3 if it is None else it * step + (n - 3))
                return sp.dma_start(dst, src)

            def load_cols(n, w_k, col, it=None, step=RING):
                if it is not None:
                    early(col * 4, it * step + (n - 3))
                load(n, raw(n).rearrange("p (k n) -> p k n", k=KD), w_k[:, :, bass.ds(col, P)],
                     it, step).then_inc(s_raw[n % RING], 16)

            def load_rows(n, w, k):
                load(n, raw(n), w[k * P:(k + 1) * P, :]).then_inc(s_raw[n % RING], 16)

            def load_mod_w(buf, i, which, col, k0=0, k1=KD):
                for m in range(2):
                    sp.dma_start(mod_slot(buf)[:, k0:k1, m, :], w_mod_k[:, k0:k1, which + m, bass.ds(col, P)])\
                        .then_inc((s_mod2 if k0 else s_mod)[i], 16)

            def load_mod_b(i, which, col):
                sp.dma_start(mod_b[0:1, i, :].rearrange("o (m n) -> o m n", m=2),
                             b_mod_m[:, which:which + 2, bass.ds(col, P)]).then_inc(s_mod[i], 16)

            def load_first(k):
                load(k, raw(k)[:, 0:896], w_in[k * P:(k + 1) * P, 128:1024]).then_inc(s_raw[k % RING], 16)

            load_mod_w(0, 0, 0, 0, 0, KD // 2)
            sp.wait_ge(s_zero, 1)
            load_mod_b(0, 0, 0)
            for t in range(TT):
                sp.dma_start(x_tok[:, t, :], x[t * P:(t + 1) * P, :]).then_inc(s_x[t], 16)
            load_mod_w(0, 0, 0, 0, KD // 2)
            for dst, src in ((V_GMIX, g_mix), (V_GFFN, g_ffn), (V_PSC, pool_scale), (V_CONV, conv_w),
                             (V_LNG, gm_ln_g), (V_LNB, gm_ln_b)):
                src = src.rearrange("o (k p) -> (o k) p", p=P)
                sp.dma_start(rows[dst - KD:dst - KD + src.shape[0], :], src).then_inc(s_vec, 16)
            load_first(0)
            for k in range(1, KD):
                if k >= 2:
                    sp.wait_ge(s_dve, (KD - 1) * (k - 2) + KD // 2)
                load_mod_w(k % 2, k % 2, 0, k * P, 0, KD // 2)
                load_mod_b(k % 2, 0, k * P)
                if k >= 2:
                    sp.wait_ge(s_acc, k - 1)
                load_mod_w(k % 2, k % 2, 0, k * P, KD // 2)
                load_first(k)
            load_cols(N_U0, w_in_k, COL_U)
            load_cols(N_XB, w_in_k, COL_XB)
            load_cols(N_XB + 1, w_in_k, COL_XB + P)
            sp.wait_ge(s_acc, KD)
            sp.dma_start(ws_raw.rearrange("p (h s) -> p h s", h=HEADS),
                         gm_w_s.rearrange("h t s -> t h s")).then_inc(s_small, 16)
            sp.dma_start(pool_sb.rearrange("p (g d) -> p g d", g=4),
                         pool_w.rearrange("g c d -> c g d")).then_inc(s_small, 16)
            sp.dma_start(bs_row, gm_b_s.rearrange("(o h) t -> o (h t)", o=1).broadcast_to((P, HEADS * P)))\
                .then_inc(s_small, 16)
            for g in range(2, 4):
                load_cols(N_XB + g, w_in_k, COL_XB + g * P)
            for cc in range(4):
                load_cols(N_CONV + 3 * cc, w_in_k, COL_CG + cc * P)
                load_cols(N_CONV + 3 * cc + 1, w_in_k, COL_HC + cc * P)
                load_cols(N_CONV + 3 * cc + 2, w_in_k, COL_BG + cc * P)

            def load_branch(j, it=None):
                n = N_C + 3
                if it is not None:
                    early(j * 4, it * 4 + (n - 3))
                sp.wait_ge(s_wlo, n - 3 if it is None else it * 4 + (n - 3))
                for b in range(3):
                    sp.dma_start(raw(n, BIG)[:, b * 512:(b + 1) * 512].rearrange("p (k n) -> p k n", k=KW),
                                 w_p_k[b][:, :, bass.ds(j, P)]).then_inc(s_raw[n % RING], 16)

            for b in range(3):
                load_cols(N_C + b, w_in_k, COL_GATE + b * D)
            load_branch(0)
            sp.wait_ge(s_gmr, HEADS)
            with sp.Fori(1, KD) as j:
                load_cols(N_C, w_in_k, j * P + COL_GATE, j)
                col = j * P - P
                need = [2 * j + (KD - i) for i in (2, 1)]
                early(4 * col, *need)
                sp.wait_ge(s_acc, need[0])
                load_mod_w(0, 0, 2, col)
                load_mod_b(0, 2, col)
                load_cols(N_C + 1, w_in_k, j * P + (COL_GATE + D), j)
                load_cols(N_C + 2, w_in_k, j * P + (COL_GATE + 2 * D), j)
                sp.wait_ge(s_acc, need[1])
                load_mod_w(0, 1, 4, col)
                load_mod_b(1, 4, col)
                load_branch(j * P, j)
            load_rows(N_WO, w_o, 0)
            sp.wait_ge(s_acc, 3 * KD - 2)
            load_mod_w(0, 0, 2, D - P)
            load_mod_b(0, 2, D - P)
            load_rows(N_WO + 1, w_o, 1)
            load_rows(N_WO + 2, w_o, 2)
            sp.wait_ge(s_acc, 3 * KD - 1)
            load_mod_w(0, 1, 4, D - P)
            load_mod_b(1, 4, D - P)
            for k in range(3, 6):
                load_rows(N_WO + k, w_o, k)
            sp.wait_ge(s_mlo, KD)
            sp.wait_ge(s_mhi, KD)
            for t in range(TT):
                sp.dma_start(x_tok[:, t, :], x[t * P:(t + 1) * P, :]).then_inc(s_x[t], 16)
            for k in range(6, KD):
                load_rows(N_WO + k, w_o, k)
            with sp.Fori(0, KF // 2) as i:
                for f in range(2):
                    for m in range(2):
                        load_cols(N_UP + 2 * f + m, w_13_k, i * (2 * P) + (m * DFF + f * P), i)
            sp.wait_ge(s_x1t, 2 * TT)
            sp.dma_start(gfin_row, g_final.rearrange("(o n) -> o n", o=1).broadcast_to((P, D))).then_inc(s_gfin, 16)
            for k in range(KF):
                load_rows(N_DOWN + k, w_2, k)
            for t in range(TT):
                for q in range(2):
                    if t < TT - 1 or q == 0:
                        sp.wait_ge(s_o, 2 * t + q + 1)
                    else:
                        sp.wait_ge(s_ol, 1)
                    sp.dma_start(out[t * P:(t + 1) * P, q * 512:(q + 1) * 512],
                                 x_tok[:, t, q * 512:(q + 1) * 512]).then_inc(s_out, 16)
            sp.wait_ge(s_out, 16 * 2 * TT)

        @block.gpsimd
        def _(pool):
            nc.gpsimd.memset(mod_b[:, :, :], 0.0).then_inc(s_zero, 1)
            nc.gpsimd.memset(ident[:, :], 0.0).then_inc(s_zero, 1)
            pool.wait_ge(s_zero, 2)
            nc.gpsimd.affine_select(out=ident[:, :], in_=ident[:, :], compare_op=ALU.not_equal, fill=1.0,
                                    base=0, pattern=[[-1, P]], channel_multiplier=1).then_inc(s_const, 1)
            nc.gpsimd.memset(half[:, :], -0.5)
            nc.gpsimd.memset(ones[:, :], 1.0)
            nc.gpsimd.memset(pads[:, :, 0:PAD], 0.0)
            for i in range(PAD):
                last = nc.gpsimd.memset(recip[:, i:i + 1], 1.0 / (i + 1))
            last.then_inc(s_const, 1)
            pool.wait_ge(s_const, 2)
            steps = 0

            def inverse_root(i, t, width, source, scale):
                nonlocal steps
                nc.gpsimd.tensor_scalar(ms[:, i, t:t + width], source, scale, EPS, ALU.mult, ALU.add)\
                    .then_inc(s_ms, 1)
                steps += 1
                pool.wait_ge(s_ms, steps)
                return nc.gpsimd.tensor_tensor(rstd[:, i, t:t + width], ms[:, i, t:t + width],
                                               half[:, t:t + width], ALU.pow)

            for t in range(TT):
                pool.wait_ge(s_ssq, t + 1)
                inverse_root(0, t, 1, ssq[:, 0, t:t + 1], 1.0 / D).then_inc(s_rstd, 1)
            def h_low(k):
                pool.wait_ge(s_hhi, k + 1)
                nc.gpsimd.tensor_tensor(h_lo[:, k, :], tmp[:, (k % 2) * 512:(k % 2 + 1) * 512],
                                        h_hi[:, k, :].bitcast(fp32), ALU.subtract).then_inc(s_hlo, 1)

            for n in range(N_U0 + 1):
                if n >= 1:
                    h_low(n - 1)
                width = 896 if n < N_U0 else SLOT
                pool.wait_ge(s_whi, n + 1)
                slab_low(nc.gpsimd, n, width)
            pool.wait_ge(s_small, 48)
            nc.gpsimd.affine_select(out=ws_raw.rearrange("p (h s) -> p h s", h=HEADS),
                                    in_=ws_raw.rearrange("p (h s) -> p h s", h=HEADS),
                                    compare_op=ALU.is_ge, fill=0.0, base=0,
                                    pattern=[[0, HEADS], [-1, P]], channel_multiplier=1).then_inc(s_mask, 1)
            pool.wait_ge(s_mv, TT)
            inverse_root(1, 0, TT, mv[:, :, 1], 1.0).then_inc(s_lnr, 1)

            def last_root(i, first):
                nonlocal steps
                t = TT - 1
                pool.wait_ge(s_ssq, first)
                nc.gpsimd.tensor_scalar(ssq[:, i, t:t + 1], ssq_last[:, 2 * i:2 * i + 1], 1.0 / D, EPS,
                                        ALU.mult, ALU.add).then_inc(s_ms, 1)
                steps += 1
                pool.wait_ge(s_ms, steps)
                pool.wait_ge(s_ssq, first + 1)
                nc.gpsimd.tensor_scalar(ms[:, i + 1, t:t + 1], ssq_last[:, 2 * i + 1:2 * i + 2], 1.0 / D,
                                        ssq[:, i, t:t + 1], ALU.mult, ALU.add).then_inc(s_ms, 1)
                steps += 1
                pool.wait_ge(s_ms, steps)
                nc.gpsimd.tensor_tensor(rstd[:, i + 1, t:t + 1], ms[:, i + 1, t:t + 1], half[:, t:t + 1],
                                        ALU.pow).then_inc(s_rstd, 1)

            for i, base in ((1, TT), (2, 2 * TT + 1)):
                for t in range(TT - 1):
                    pool.wait_ge(s_ssq, base + t + 1)
                    inverse_root(i + 1, t, 1, ssq[:, i, t:t + 1], 1.0 / D).then_inc(s_rstd, 1)
                    if i == 1 and t == 1:
                        for m in range(2):
                            pool.wait_ge(s_h2hi, m + 1)
                            tile_low(nc.gpsimd, m)
                if i == 1:
                    pool.wait_ge(s_wlo, N_UP + 2)
                    pool.wait_ge(s_whi, N_UP + 3)
                    slab_low(nc.gpsimd, N_UP + 2)
                last_root(i, base + TT)

        @block.scalar
        def _(act):
            def split_hi(n, it=None, step=RING, width=SLOT):
                big = n >= N_C + 3 and n <= N_WO - 1 and (n - N_C) % 4 == 3
                s = n % RING
                before = 16 * (n // RING + 1)
                each = 16
                if s == 0:
                    first = (N_C + 3) // RING
                    extra = min(max(n // RING + 1 - first, 0), KD) * 32
                    before += extra
                    if it is not None and big:
                        each = 48
                act.wait_ge(s_raw[s], before if it is None else it * each + before)
                if n >= RING:
                    act.wait_ge(s_used, n - 3 if it is None else it * step + (n - 3))
                nc.scalar.activation(hi(n, width), raw(n, width), ACT.Copy).then_inc(s_whi, 1)

            act.dma_start(c_rows, c.rearrange("o (k p) -> (o k) p", p=P)).then_inc(s_cl, 16)
            act.wait_ge(s_vecsb, 1)
            nc.scalar.activation(c_act[:, :], vec[:, V_C:V_C + KD], ACT.Silu).then_inc(s_c, 1)

            def square(t, i):
                if t >= 1:
                    act.wait_ge(s_ssq, t)
                nc.scalar.activation(tmp[:, :], x_tok[:, t, :], ACT.Square,
                                     accum_out=ssq[:, i, t:t + 1]).then_inc(s_ssq, 1)

            def x_copy(t, q):
                act.wait_ge(s_xt, 2 * t + q + 1)
                nc.scalar.activation(x_tok[:, t, q * 512:(q + 1) * 512], ps[2 * (t % 3) + q][:, :], ACT.Copy)\
                    .then_inc(s_xta, 1)

            for t in range(TT):
                act.wait_ge(s_x[t], 16)
                square(t, 0)
            for t in range(2):
                for q in range(2):
                    x_copy(t, q)
            split_hi(0, width=896)
            x_copy(2, 0)
            x_copy(2, 1)
            x_copy(3, 0)

            def h_block(k):
                act.wait_ge(s_ab, k + 1)
                act.wait_ge(s_xtd, 1)
                act.wait_ge(s_xta, 7)
                if k >= 2:
                    act.wait_ge(s_hlo, k - 1)
                buf = tmp[:, (k % 2) * 512:(k % 2 + 1) * 512]
                nc.scalar.activation(buf.rearrange("p (t s) -> p t s", t=TT), x_tok[:, :, k * P:(k + 1) * P],
                                     ACT.Identity, bias=b1[:, k:k + 1], scale=a1[:, k:k + 1]).then_inc(s_h, 1)
                act.wait_ge(s_h, k + 1)
                nc.scalar.activation(h_hi[:, k, :], buf, ACT.Copy).then_inc(s_hhi, 1)

            h_block(0)
            split_hi(1, width=896)
            for k in range(KD - 1):
                split_hi(k + 2, width=896 if k + 2 < KD else SLOT)
                h_block(k + 1)
            split_hi(N_U0 + 1)

            split_hi(N_U0 + 2)
            for t in range(TT):
                act.wait_ge(s_first, t + 1)
                nc.scalar.activation(v_tok[t], ps[t][:, :], ACT.Gelu_apprx_tanh).then_inc(s_vg, 1)
            for i in range(1, HEADS):
                if i < HEADS - 1:
                    act.wait_ge(s_first, TT + i)
                else:
                    act.wait_ge(s_used, KD)
                nc.scalar.activation(u_gelu[i], ps[3 + i][:, :], ACT.Gelu_apprx_tanh).then_inc(s_ug, 1)
            act.wait_ge(s_used, N_U0 + 1)
            nc.scalar.activation(u_gelu[0], ps[7][:, :], ACT.Gelu_apprx_tanh).then_inc(s_ug, 1)

            def xb_copy(g):
                act.wait_ge(s_used, N_XB + g + 1)
                if g >= 1:
                    act.wait_ge(s_p, g)
                nc.scalar.activation(pads[:, 0, PAD:PAD + SEQ], ps[g][:, :], ACT.Copy).then_inc(s_xb, 1)

            def yb_hi(g):
                act.wait_ge(s_pm, g + 1)
                nc.scalar.activation(act_hi[:, YB + g, :], ps[7][:, :], ACT.Copy,
                                     scale=vec[:, V_PSC + g:V_PSC + g + 1]).then_inc(s_ybhi, 1)

            def cg_copy(cc):
                act.wait_ge(s_used, N_CONV + 3 * cc + 1)
                if cc >= 1:
                    act.wait_ge(s_z, cc)
                nc.scalar.activation(cg_sb, ps[3 * cc % 6][:, :], ACT.Copy).then_inc(s_cg, 1)

            def ya_hi(h):
                act.wait_ge(s_ya, h + 1)
                nc.scalar.activation(act_hi[:, YA + h, :], pads[:, 2, PAD:PAD + SEQ], ACT.Copy).then_inc(s_yahi, 1)

            def yc_hi(cc):
                act.wait_ge(s_yc, cc + 1)
                nc.scalar.activation(act_hi[:, YC + cc, :], yc_sb, ACT.Copy).then_inc(s_ychi, 1)

            todo = {0: [(xb_copy, 0)], 1: [(xb_copy, 1)], 2: [(xb_copy, 2), (yb_hi, 0)],
                    3: [(xb_copy, 3), (yb_hi, 1)], 4: [(cg_copy, 0), (ya_hi, 0)], 5: [(yb_hi, 2)],
                    6: [(yc_hi, 0), (ya_hi, 1)], 7: [(cg_copy, 1), (yb_hi, 3)], 8: [(ya_hi, 2)],
                    9: [(yc_hi, 1)], 10: [(cg_copy, 2), (ya_hi, 3)], 12: [(yc_hi, 2)],
                    13: [(cg_copy, 3)], 15: [(yc_hi, 3)]}
            for n in range(N_XB, N_C):
                split_hi(n + AHEAD)
                for step, i in todo.get(n - N_XB, []):
                    step(i)

            def gate_copy(row, pair, j):
                act.wait_ge(s_red, 2 * j + (KD + pair + 1))
                nc.scalar.activation(gate_row[row][:, bass.ds(j * P, P)], ps[4][:, 0:P], ACT.Copy)\
                    .then_inc(s_row, 1)

            with act.Fori(0, KD) as j:
                for b in range(3):
                    n = N_C + b
                    split_hi(n + AHEAD, it=j, width=BIG if b == 1 else SLOT)
                    act.wait_ge(s_used, j * 4 + (n + 1))
                    act.wait_ge(s_ab, j * 2 + KD)
                    nc.scalar.activation(sig[b], ps[b][:, :], ACT.Sigmoid).then_inc(s_sig, 1)
                split_hi(N_C + 3 + AHEAD, it=j)
                act.wait_ge(s_yclo, 4)
                gate_copy(0, 0, j)
                act.wait_ge(s_m, j + 1)
                nc.scalar.activation(act_hi[:, bass.ds(j + MERGED, 1), :], merge[0], ACT.Copy).then_inc(s_mhi, 1)
                gate_copy(1, 1, j)

            for n in range(N_WO + AHEAD, N_UP):
                split_hi(n)

            def square1(t):
                act.wait_ge(s_x1, t + 1)
                if t >= 2:
                    act.wait_ge(s_x1t, 2 * (t - 1))
                nc.scalar.activation(x1n[t % 2], x_tok[:, t, :], ACT.Square,
                                     accum_out=ssq[:, 1, t:t + 1]).then_inc(s_ssq, 1)

            def square1_last(q):
                act.wait_ge(s_x1, TT + q)
                act.wait_ge(s_x1t, 2 * (TT - 2))
                nc.scalar.activation(x1n[1][:, q * 512:(q + 1) * 512], x_tok[:, TT - 1, q * 512:(q + 1) * 512],
                                     ACT.Square, accum_out=ssq_last[:, 2 + q:3 + q]).then_inc(s_ssq, 1)

            def h2_part(t):
                act.wait_ge(s_x1t, 2 * t + 1)
                if t >= 1:
                    act.wait_ge(s_h2lo, t)
                for k in range(4):
                    last = nc.scalar.activation(h2_tmp[:, k * P:(k + 1) * P], ps[2 * t][:, k * P:(k + 1) * P],
                                                ACT.Identity, bias=cols2[:, 0, k:k + 1], scale=a2[:, k:k + 1])
                last.then_inc(s_h2a, 1)

            def h2_high(t):
                act.wait_ge(s_h2a, t + 1)
                act.wait_ge(s_h2d, t + 1)
                nc.scalar.activation(h_hi[:, :, t * P:(t + 1) * P], h2_tmp.rearrange("p (k s) -> p k s", k=KD),
                                     ACT.Copy).then_inc(s_h2hi, 1)

            square1(0)
            h2_part(0)
            square1(1)
            h2_high(0)
            h2_part(1)
            h2_high(1)
            split_hi(N_UP)
            square1(2)
            split_hi(N_UP + 1)
            split_hi(N_UP + 2)
            split_hi(N_UP + 3)
            square1_last(0)
            square1_last(1)
            h2_part(2)
            h2_high(2)
            h2_part(3)
            h2_high(3)

            def silu(f, it=None):
                act.wait_ge(s_used, N_UP + 2 * f + 1 if it is None else it * 4 + (N_UP + 2 * f + 1))
                if it is not None:
                    act.wait_ge(s_g, it * 2 + (f - 1))
                nc.scalar.activation(pads[:, f, 0:512], ps[2 * f][:, :], ACT.Silu).then_inc(s_a, 1)

            def hidden_hi(f, it=None):
                act.wait_ge(s_g, f + 1 if it is None else it * 2 + (f + 1))
                at = f if it is None else bass.ds(it * 2 + f, 1)
                nc.scalar.activation(act_hi[:, at, :], tmp[:, f * 512:(f + 1) * 512], ACT.Copy).then_inc(s_ghi, 1)

            silu(0)
            split_hi(N_UP + 4)
            hidden_hi(0)
            split_hi(N_UP + 5)
            silu(1)
            hidden_hi(1)
            with act.Fori(1, KF // 2) as i:
                for f in range(2):
                    n = N_UP + 2 * f
                    split_hi(n + AHEAD, it=i)
                    silu(f, i)
                    split_hi(n + 1 + AHEAD, it=i)
                    hidden_hi(f, i)

            for n in range(N_DOWN + AHEAD, N_END):
                split_hi(n)
            for t in range(TT - 1):
                act.wait_ge(s_x2, t + 1)
                if t >= 1:
                    act.wait_ge(s_ssq, 2 * TT + 1 + t)
                nc.scalar.activation(pads[:, 0:2, 0:512], x_tok[:, t, :].rearrange("p (a b) -> p a b", a=2),
                                     ACT.Square, accum_out=ssq[:, 2, t:t + 1]).then_inc(s_ssq, 1)
            act.wait_ge(s_ssq, 3 * TT)
            for q in range(2):
                act.wait_ge(s_x2, TT + q)
                nc.scalar.activation(pads[:, q, 0:512], x_tok[:, TT - 1, q * 512:(q + 1) * 512],
                                     ACT.Square, accum_out=ssq_last[:, 4 + q:5 + q]).then_inc(s_ssq, 1)
            act.wait_ge(s_xg, 2)
            act.wait_ge(s_rstd, 3 * TT)
            nc.scalar.activation(x_tok[:, TT - 1, 512:D], tmp[:, 512:D], ACT.Copy,
                                 scale=rstd[:, 3, TT - 1:TT]).then_inc(s_ol, 1)

        @block.vector
        def _(dve):
            part = {"first": 0, "each": 0, "it": None, "steps": 0}

            def link(ins, meanwhile=None):
                part["steps"] += 1
                ins.then_inc(s_dve, 1)
                if meanwhile:
                    meanwhile()
                n = part["first"] + part["steps"]
                dve.wait_ge(s_dve, n if part["it"] is None else part["it"] * part["each"] + n)

            def split_lo(n, it=None, step=RING, width=SLOT):
                dve.wait_ge(s_whi, n + 1 if it is None else it * step + (n + 1))
                slab_low(nc.vector, n, width)

            dve.wait_ge(s_vect, 1)
            nc.vector.tensor_copy(vec[:, 0:KD], ps[6][:, 0:KD]).then_inc(s_vecsb, 1)

            def x_copy(t):
                dve.wait_ge(s_xt, 2 * t + 2)
                nc.vector.tensor_copy(x_tok[:, t, 512:1024], ps[2 * (t % 3) + 1][:, :]).then_inc(s_xtd, 1)

            def x_norm(t):
                dve.wait_ge(s_rstd, t + 1)
                nc.vector.tensor_scalar(x_tok[:, t, :], x_tok[:, t, :], rstd[:, 0, t:t + 1], None, ALU.mult)\
                    .then_inc(s_xn, 1)

            def mod_pair(v, buf, i, it=None, landed=None, landed2=None, meanwhile=None):
                dve.wait_ge(s_mod[i], landed)
                if it is not None or v >= 2:
                    dve.wait_ge(s_red, v - 1 if it is None else it * 2 + (v - 1))
                acc = mod_acc[:, i, :]
                piece = mod_w[:, buf * 2048:(buf + 1) * 2048].rearrange("p (k n) -> p k n", k=KD)
                for k in range(KD):
                    if k == KD // 2 and landed2 is not None:
                        dve.wait_ge(s_mod2[i], landed2)
                    ins = nc.vector.scalar_tensor_tensor(out=acc, in0=piece[:, k, :], scalar=c_act[:, k:k + 1],
                                                         in1=acc if k else mod_b[:, i, :],
                                                         op0=ALU.mult, op1=ALU.add)
                    if k < KD - 1:
                        link(ins, (meanwhile or {}).get(k))
                ins.then_inc(s_acc, 1)

            def columns1(k):
                dve.wait_ge(s_red, k + 1)
                nc.vector.tensor_copy(b1[:, k:k + 1], ps[7][:, 0:1])
                nc.vector.scalar_tensor_tensor(out=a1[:, k:k + 1], in0=ps[7][:, 1:2], scalar=1.0,
                                               in1=vec[:, V_GMIX + k:V_GMIX + k + 1],
                                               op0=ALU.add, op1=ALU.mult).then_inc(s_ab, 1)

            def first_tiles():
                for t in range(3):
                    x_norm(t)

            dve.wait_ge(s_c, 1)
            mod_pair(0, 0, 0, landed=48, landed2=32,
                     meanwhile={3: first_tiles, 4: lambda: x_norm(3)})
            dve.wait_ge(s_vect, 2)
            nc.vector.tensor_copy(vec[:, KD:V_END], ps[6][:, KD:V_END]).then_inc(s_vecsb, 1)
            x_copy(3)
            dve.wait_ge(s_vecsb, 2)
            columns1(0)
            for v in range(1, KD):
                mod_pair(v, v % 2, v % 2, landed=48 * (v // 2 + 1), landed2=32 * (v // 2 + 1),
                         meanwhile={2: lambda: columns1(v - 1)} if v >= 2 else None)
            columns1(KD - 1)
            dve.wait_ge(s_wlo, N_U0 + 1)
            split_lo(N_U0 + 1)

            split_lo(N_U0 + 2)
            for t in range(TT):
                dve.wait_ge(s_vg, t + 1)
                link(nc.vector.bn_stats(stats[:, t, :], v_tok[t]))
                nc.vector.bn_aggr(mv[:, t, :], stats[:, t, :]).then_inc(s_mv, 1)

            def v_norm():
                dve.wait_ge(s_lnr, 1)
                for t in range(TT):
                    nc.vector.tensor_scalar(v_tok[t], v_tok[t], mv[:, t, 0:1], rstd[:, 1, t:t + 1],
                                            ALU.subtract, ALU.mult).then_inc(s_vn, 1)

            def pool(g):
                win = WINDOWS[g]
                dve.wait_ge(s_xb, g + 1)
                src = 0
                for lev in range(g + 1):
                    lag = 1 << lev
                    dst = 1 + lev % 2
                    link(nc.vector.tensor_tensor(pads[:, dst, PAD:PAD + SEQ], pads[:, src, PAD:PAD + SEQ],
                                                 pads[:, src, PAD - lag:PAD + SEQ - lag], ALU.add))
                    src = dst
                if g >= 2:
                    dve.wait_ge(s_pm, g - 1)
                p = tmp[:, (g % 2) * 512:(g % 2 + 1) * 512]
                link(nc.vector.tensor_tensor(fix[:, 0:win - 1], pads[:, src, PAD:PAD + win - 1],
                                             recip[:, 0:win - 1], ALU.mult))
                nc.vector.scalar_tensor_tensor(out=p[:, win - 1:SEQ], in0=pads[:, src, PAD + win - 1:PAD + SEQ],
                                               scalar=1.0 / win, in1=pads[:, 0, PAD + win - 1:PAD + SEQ],
                                               op0=ALU.mult, op1=ALU.subtract)
                nc.vector.tensor_tensor(p[:, 0:win - 1], fix[:, 0:win - 1], pads[:, 0, PAD:PAD + win - 1],
                                        ALU.subtract).then_inc(s_p, 1)

            def ws_copy():
                dve.wait_ge(s_wst, 1)
                nc.vector.tensor_copy(ws_t, ps[6][:, :]).then_inc(s_wsc, 1)

            def bias_rows():
                dve.wait_ge(s_rs, 1)
                for h in range(HEADS):
                    last = nc.vector.scalar_tensor_tensor(
                        out=gate_bias[:, h * P:(h + 1) * P], in0=ps[6][:, h * P:(h + 1) * P],
                        scalar=vec[:, V_LNB + h:V_LNB + h + 1], in1=bs_row[:, h * P:(h + 1) * P],
                        op0=ALU.mult, op1=ALU.add)
                last.then_inc(s_gb, 1)

            def yb_low(g):
                dve.wait_ge(s_ybhi, g + 1)
                nc.vector.scalar_tensor_tensor(out=act_lo[:, YB + g, :], in0=ps[7][:, :],
                                               scalar=vec[:, V_PSC + g:V_PSC + g + 1],
                                               in1=act_hi[:, YB + g, :].bitcast(fp32),
                                               op0=ALU.mult, op1=ALU.subtract).then_inc(s_yblo, 1)

            def gating(h):
                dve.wait_ge(s_gm, h + 1)
                dve.wait_ge(s_p, 4)
                s = pads[:, 2, PAD:PAD + SEQ]
                bias = gate_bias[:, h * P:(h + 1) * P].rearrange("p (o t) -> p o t", o=1).broadcast_to((P, TT, P))
                nc.vector.scalar_tensor_tensor(out=s.rearrange("p (n t) -> p n t", n=TT),
                                               in0=ps[6][:, :].rearrange("p (n t) -> p n t", n=TT),
                                               scalar=vec[:, V_LNG + h:V_LNG + h + 1], in1=bias,
                                               op0=ALU.mult, op1=ALU.add).then_inc(s_gmr, 1)
                dve.wait_ge(s_gmr, h + 1)
                dve.wait_ge(s_ug, 4)
                nc.vector.tensor_tensor(s, s, u_gelu[h], ALU.mult).then_inc(s_ya, 1)
                dve.wait_ge(s_yahi, h + 1)
                nc.vector.tensor_tensor(act_lo[:, YA + h, :], s, act_hi[:, YA + h, :].bitcast(fp32),
                                        ALU.subtract)

            def conv(cc):
                z = pads[:, cc % 2, :]
                dve.wait_ge(s_used, N_CONV + 3 * cc + 2)
                dve.wait_ge(s_cg, cc + 1)
                dve.wait_ge(s_p, 4)
                nc.vector.tensor_tensor(z[:, PAD:PAD + SEQ], ps[(3 * cc + 1) % 6][:, :], cg_sb, ALU.mult)\
                    .then_inc(s_z, 1)
                dve.wait_ge(s_z, cc + 1)
                w = [vec[:, V_CONV + 4 * i + cc:V_CONV + 4 * i + cc + 1] for i in range(3)]
                link(nc.vector.tensor_scalar(taps, z[:, PAD - 2:PAD - 2 + SEQ], w[0], None, ALU.mult))
                for i in (1, 2):
                    link(nc.vector.scalar_tensor_tensor(out=taps, in0=z[:, PAD - 2 + i:PAD - 2 + i + SEQ],
                                                        scalar=w[i], in1=taps, op0=ALU.mult, op1=ALU.add))

            def conv_gate(cc):
                dve.wait_ge(s_used, N_CONV + 3 * cc + 3)
                nc.vector.tensor_tensor(yc_sb, ps[(3 * cc + 2) % 6][:, :], taps, ALU.mult).then_inc(s_yc, 1)
                dve.wait_ge(s_ychi, cc + 1)
                nc.vector.tensor_tensor(act_lo[:, YC + cc, :], yc_sb, act_hi[:, YC + cc, :].bitcast(fp32),
                                        ALU.subtract).then_inc(s_yclo, 1)

            todo = {0: [(v_norm,), (pool, 0)], 1: [(pool, 1), (ws_copy,)], 2: [(pool, 2), (bias_rows,), (yb_low, 0)],
                    3: [(pool, 3), (yb_low, 1)], 4: [(gating, 0)], 5: [(conv, 0), (yb_low, 2)],
                    6: [(conv_gate, 0), (gating, 1)], 7: [(yb_low, 3)], 8: [(conv, 1), (gating, 2)],
                    9: [(conv_gate, 1)], 10: [(gating, 3)], 11: [(conv, 2)], 12: [(conv_gate, 2)],
                    14: [(conv, 3)], 15: [(conv_gate, 3)]}
            for n in range(N_XB, N_C):
                split_lo(n + AHEAD)
                for step, *i in todo.get(n - N_XB, []):
                    step(*i)

            part["first"] += part["steps"]
            links = 2 * (KD - 1) + 1
            with dve.Fori(0, KD) as j:
                part.update(it=j, each=links, steps=0)
                split_lo(N_C + AHEAD, it=j)
                mod_pair(KD, 0, 0, it=j, landed=j * 48 + 48 * (KD // 2 + 1))
                split_lo(N_C + 1 + AHEAD, it=j, width=BIG)
                split_lo(N_C + 2 + AHEAD, it=j)
                mod_pair(KD + 1, 0, 1, it=j, landed=j * 48 + 48 * (KD // 2 + 1))
                split_lo(N_C + 3 + AHEAD, it=j)
                dve.wait_ge(s_red, j * 2 + (KD + 1))
                nc.vector.tensor_copy(cols2[:, 0, bass.ds(j, 1)], ps[3][:, 0:1]).then_inc(s_ab, 1)
                dve.wait_ge(s_sig, j * 3 + 3)
                for b in range(3):
                    if b < 2:
                        dve.wait_ge(s_yp, j * 2 + (b + 1))
                    else:
                        dve.wait_ge(s_used, j * 4 + (N_C + 4))
                    nc.vector.tensor_tensor(merge[min(b, 1)], ps[5 + b][:, :], sig[b], ALU.mult).then_inc(s_y, 1)
                    dve.wait_ge(s_y, j * 3 + (b + 1))
                    if b == 1:
                        link(nc.vector.tensor_tensor(merge[0], merge[0], merge[1], ALU.add))
                    if b == 2:
                        nc.vector.tensor_tensor(merge[0], merge[0], merge[1], ALU.add).then_inc(s_m, 1)
                dve.wait_ge(s_mhi, j + 1)
                nc.vector.tensor_tensor(act_lo[:, bass.ds(j + MERGED, 1), :], merge[0],
                                        act_hi[:, bass.ds(j + MERGED, 1), :].bitcast(fp32),
                                        ALU.subtract).then_inc(s_mlo, 1)
                dve.wait_ge(s_red, j * 2 + (KD + 2))
                nc.vector.tensor_copy(cols2[:, 1, bass.ds(j, 1)], ps[3][:, 0:1]).then_inc(s_ab, 1)
            assert part["steps"] == links
            part.update(it=None, first=part["first"] + KD * links, steps=0)

            dve.wait_ge(s_ab, 3 * KD)
            link(nc.vector.scalar_tensor_tensor(out=a2[:, :], in0=cols2[:, 1, :], scalar=1.0,
                                                in1=vec[:, V_GFFN:V_GFFN + KD], op0=ALU.add, op1=ALU.mult))
            for n in range(N_WO + AHEAD, N_UP):
                split_lo(n)

            def residual(t, done, used, row, ready):
                if t < TT - 1 or done is s_dn:
                    dve.wait_ge(done, t + 1)
                else:
                    dve.wait_ge(s_used, used)
                if t >= 1:
                    dve.wait_ge(ready, t)
                for q in range(2):
                    cols = slice(q * 512, (q + 1) * 512)
                    if t == TT - 1 and q == 1:
                        dve.wait_ge(s_used, used)
                    ins = nc.vector.tensor_tensor(tmp[:, cols], ps[2 * t + q][:, :], row[:, cols], ALU.mult)
                    if t == TT - 1:
                        link(ins)
                        nc.vector.tensor_tensor(x_tok[:, t, cols], x_tok[:, t, cols], tmp[:, cols], ALU.add)\
                            .then_inc(ready, 1)
                if t < TT - 1:
                    link(ins)
                    nc.vector.tensor_tensor(x_tok[:, t, :], x_tok[:, t, :], tmp[:, :], ALU.add).then_inc(ready, 1)

            def x1_tile(t):
                if t == 0:
                    dve.wait_ge(s_row, 2 * KD)
                dve.wait_ge(s_x[t], 32)
                residual(t, s_wo, N_UP, gate_row[0], s_x1)

            def x1_norm(t):
                dve.wait_ge(s_rstd, TT + t + 1)
                nc.vector.tensor_scalar(x1n[t % 2], x_tok[:, t, :], rstd[:, 2, t:t + 1], None, ALU.mult)\
                    .then_inc(s_x1n, 1)

            def h2_part(t):
                dve.wait_ge(s_x1t, 2 * t + 2)
                if t >= 1:
                    dve.wait_ge(s_h2lo, t)
                for k in range(4, KD):
                    last = nc.vector.tensor_scalar(h2_tmp[:, k * P:(k + 1) * P],
                                                   ps[2 * t + 1][:, (k - 4) * P:(k - 3) * P],
                                                   a2[:, k:k + 1], cols2[:, 0, k:k + 1], ALU.mult, ALU.add)
                last.then_inc(s_h2d, 1)

            def h2_low(t):
                dve.wait_ge(s_h2hi, t + 1)
                tile_low(nc.vector, t)

            x1_tile(0)
            x1_norm(0)
            x1_tile(1)
            h2_part(0)
            x1_norm(1)
            h2_part(1)
            x1_tile(2)
            split_lo(N_UP)
            x1_norm(2)
            split_lo(N_UP + 1)
            x1_tile(3)
            h2_part(2)
            x1_norm(3)
            dve.wait_ge(s_wlo, N_UP + 3)
            split_lo(N_UP + 3)
            dve.wait_ge(s_h2lo, 2)
            h2_low(2)
            h2_part(3)
            h2_low(3)

            def hidden(f, it=None):
                dve.wait_ge(s_used, N_UP + 2 * f + 2 if it is None else it * 4 + (N_UP + 2 * f + 2))
                dve.wait_ge(s_a, f + 1 if it is None else it * 2 + (f + 1))
                nc.vector.tensor_tensor(tmp[:, f * 512:(f + 1) * 512], ps[2 * f + 1][:, :], pads[:, f, 0:512],
                                        ALU.mult).then_inc(s_g, 1)

            def hidden_low(f, it=None):
                dve.wait_ge(s_ghi, f + 1 if it is None else it * 2 + (f + 1))
                at = slice(f, f + 1) if it is None else bass.ds(it * 2 + f, 1)
                nc.vector.tensor_tensor(act_lo[:, at, :], tmp[:, f * 512:(f + 1) * 512],
                                        act_hi[:, at, :].bitcast(fp32), ALU.subtract).then_inc(s_glo, 1)

            split_lo(N_UP + 4)
            hidden(0)
            hidden_low(0)
            split_lo(N_UP + 5)
            hidden(1)
            hidden_low(1)
            with dve.Fori(1, KF // 2) as i:
                for f in range(2):
                    n = N_UP + 2 * f
                    split_lo(n + AHEAD, it=i)
                    split_lo(n + 1 + AHEAD, it=i)
                    hidden(f, i)
                    hidden_low(f, i)

            for n in range(N_DOWN + AHEAD, N_END):
                split_lo(n)
            dve.wait_ge(s_gfin, 16)

            def out_tile(t):
                dve.wait_ge(s_rstd, 2 * TT + t + 1)
                for q in range(2):
                    part_x = x_tok[:, t, q * 512:(q + 1) * 512]
                    nc.vector.scalar_tensor_tensor(out=part_x, in0=part_x, scalar=rstd[:, 3, t:t + 1],
                                                   in1=gfin_row[:, q * 512:(q + 1) * 512],
                                                   op0=ALU.mult, op1=ALU.mult).then_inc(s_o, 1)

            for t in range(TT):
                residual(t, s_dn, N_END, gate_row[1], s_x2)
                if t >= 1:
                    out_tile(t - 1)
            dve.wait_ge(s_x2, TT + 1)
            for q in range(2):
                cols = slice(q * 512, (q + 1) * 512)
                nc.vector.tensor_tensor(tmp[:, cols], x_tok[:, TT - 1, cols], gfin_row[:, cols], ALU.mult)\
                    .then_inc(s_xg, 1)
            dve.wait_ge(s_xg, 1)
            dve.wait_ge(s_rstd, 3 * TT)
            nc.vector.tensor_scalar(x_tok[:, TT - 1, 0:512], tmp[:, 0:512], rstd[:, 3, TT - 1:TT], None, ALU.mult)\
                .then_inc(s_o, 1)

        @block.tensor
        def _(pe):
            def three(dst, w, m, start, stop):
                nc.tensor.matmul(dst, w[0], m[0], start=start, stop=False)
                nc.tensor.matmul(dst, w[1], m[0], start=False, stop=False)
                return nc.tensor.matmul(dst, w[0], m[1], start=False, stop=stop)

            def weights(n, a, width=P):
                return hi(n, BIG if n % RING == 0 else SLOT)[:, a:a + width], \
                    lo(n, BIG if n % RING == 0 else SLOT)[:, a:a + width]

            def slab_ready(n, it=None, step=RING):
                pe.wait_ge(s_whi, n + 1 if it is None else it * step + (n + 1))
                pe.wait_ge(s_wlo, n + 1 if it is None else it * step + (n + 1))

            def hT(k, a=0, b=SEQ):
                return h_hi[:, k, a:b], h_lo[:, k, a:b]

            def acts(k, a=0, b=SEQ):
                return act_hi[:, k, a:b], act_lo[:, k, a:b]

            def project(n, bank, it=None, a=0, b=SEQ, used=True):
                slab_ready(n, it)
                for k in range(KD):
                    last = three(ps[bank][:, a:b], weights(n, k * P), hT(k, a, b), k == 0, k == KD - 1)
                if used:
                    last.then_inc(s_used, 1)

            def column(dst, bias, m):
                return nc.tensor.matmul(dst, mod_acc[:, bias, m * P:(m + 1) * P], ones[:, 0:1],
                                        start=True, stop=True)

            def row(dst, bias, m):
                return nc.tensor.matmul(dst, ones[:, :], mod_acc[:, bias, m * P:(m + 1) * P],
                                        start=True, stop=True)

            def reduce1(k):
                pe.wait_ge(s_acc, k + 1)
                if k >= 1:
                    pe.wait_ge(s_ab, k)
                column(ps[7][:, 0:1], k % 2, 0)
                column(ps[7][:, 1:2], k % 2, 1).then_inc(s_red, 1)

            pe.wait_ge(s_const, 2)
            pe.wait_ge(s_cl, 16)
            nc.tensor.transpose(ps[6][:, 0:KD], c_rows, ident[0:KD, 0:KD]).then_inc(s_vect, 1)
            for t in range(TT):
                if t == TT - 1:
                    pe.wait_ge(s_vec, 6 * 16)
                    pe.wait_ge(s_vecsb, 1)
                    nc.tensor.transpose(ps[6][:, KD:V_END], rows[0:V_END - KD, :],
                                        ident[0:V_END - KD, 0:V_END - KD]).then_inc(s_vect, 1)
                pe.wait_ge(s_xn, t + 1)
                if t == 3:
                    pe.wait_ge(s_xta, 2)
                for q in range(2):
                    for i in range(4):
                        k = 4 * q + i
                        last = nc.tensor.transpose(ps[2 * (t % 3) + q][:, i * P:(i + 1) * P],
                                                   x_tok[:, t, k * P:(k + 1) * P], ident[:, :])
                    last.then_inc(s_xt, 1)

            reduce1(0)

            pe.wait_ge(s_vecsb, 2)
            pe.wait_ge(s_xta, 7)
            pe.wait_ge(s_xtd, 1)
            V0 = COL_V - P

            def product(k, i):
                if i < TT:
                    return (h_hi[:, k, i * P:(i + 1) * P], h_lo[:, k, i * P:(i + 1) * P]), \
                        weights(k, V0, 512)
                return weights(k, (i - 4) * P), hT(k)

            for k in range(KD):
                pe.wait_ge(s_whi, k + 1)
                pe.wait_ge(s_hhi, k + 1)
                if k < KD - 1:
                    for i in range(7):
                        w, m = product(k, i)
                        nc.tensor.matmul(ps[i][:, :], w[0], m[0], start=k == 0, stop=False)
                    pe.wait_ge(s_wlo, k + 1)
                    for i in range(7):
                        if i == 3:
                            reduce1(k + 1)
                        w, m = product(k, i)
                        nc.tensor.matmul(ps[i][:, :], w[1] if i >= TT else w[0], m[0] if i >= TT else m[1],
                                         start=False, stop=False)
                    pe.wait_ge(s_hlo, k + 1)
                    for i in range(7):
                        w, m = product(k, i)
                        last = nc.tensor.matmul(ps[i][:, :], w[0] if i >= TT else w[1],
                                                m[1] if i >= TT else m[0], start=False, stop=False)
                    last.then_inc(s_used, 1)
                else:
                    for i in range(7):
                        w, m = product(k, i)
                        nc.tensor.matmul(ps[i][:, :], w[0], m[0], start=False, stop=False)
                    pe.wait_ge(s_wlo, k + 1)
                    pe.wait_ge(s_hlo, k + 1)
                    for i in range(7):
                        w, m = product(k, i)
                        nc.tensor.matmul(ps[i][:, :], w[1], m[0], start=False, stop=False)
                        nc.tensor.matmul(ps[i][:, :], w[0], m[1], start=False, stop=True)\
                            .then_inc(s_first if i < 6 else s_used, 1)

            def ws_transpose():
                pe.wait_ge(s_mask, 1)
                pe.wait_ge(s_ug, 3)
                for h in range(HEADS):
                    last = nc.tensor.transpose(ps[6][:, h * P:(h + 1) * P], ws_raw[:, h * P:(h + 1) * P],
                                               ident[:, :])
                last.then_inc(s_wst, 1)

            def ws_rowsum():
                pe.wait_ge(s_wsc, 1)
                nc.tensor.matmul(ps[6][:, :], ones[:, :], ws_t, start=True, stop=True).then_inc(s_rs, 1)

            def pool_map(g):
                pe.wait_ge(s_p, g + 1)
                if g == 0:
                    pe.wait_ge(s_ug, 4)
                else:
                    pe.wait_ge(s_yblo, g)
                nc.tensor.matmul(ps[7][:, :], pool_sb[:, g * P:(g + 1) * P], tmp[:, (g % 2) * 512:(g % 2 + 1) * 512],
                                 start=True, stop=True).then_inc(s_pm, 1)

            def gate_tokens(h):
                if h == 0:
                    pe.wait_ge(s_gb, 1)
                    pe.wait_ge(s_vn, TT)
                else:
                    pe.wait_ge(s_gmr, h)
                for t in range(TT):
                    last = nc.tensor.matmul(ps[6][:, t * P:(t + 1) * P], v_tok[t][:, h * P:(h + 1) * P],
                                            ws_t[:, h * P:(h + 1) * P], start=True, stop=True)
                last.then_inc(s_gm, 1)

            pe.wait_ge(s_ab, KD)
            project(N_U0, 7)
            todo = {1: [(ws_transpose,)], 2: [(ws_rowsum,), (pool_map, 0)], 3: [(pool_map, 1)],
                    4: [(gate_tokens, 0)], 5: [(pool_map, 2)], 6: [(gate_tokens, 1)],
                    7: [(pool_map, 3)], 8: [(gate_tokens, 2)], 10: [(gate_tokens, 3)]}
            for n in range(N_XB, N_C):
                if n < N_CONV:
                    bank = n - N_XB
                    pe.wait_ge(s_vg, bank + 1)
                else:
                    m = n - N_CONV
                    bank = m % 6
                    if m < 4:
                        pe.wait_ge(s_xb, m + 1)
                    elif m >= 6:
                        pe.wait_ge((s_cg, s_z, s_yc)[m % 3], m // 3 - 1)
                project(n, bank)
                for step, *i in todo.get(n - N_XB, []):
                    step(*i)

            pe.wait_ge(s_cg, 3)
            pe.wait_ge(s_z, 3)
            pe.wait_ge(s_yc, 3)
            with pe.Fori(0, KD) as j:
                for b in range(3):
                    project(N_C + b, b, it=j)
                pe.wait_ge(s_acc, j * 2 + (KD + 1))
                pe.wait_ge(s_ab, j * 2 + KD)
                pe.wait_ge(s_yc, 4)
                column(ps[3][:, 0:1], 0, 1)
                row(ps[4][:, 0:P], 0, 0).then_inc(s_red, 1)
                slab_ready(N_C + 3, it=j)
                pe.wait_ge(s_yblo, 4)
                pe.wait_ge(s_yclo, 4)
                for b, first in enumerate((YA, YB, YC)):
                    for k in range(KW):
                        last = three(ps[5 + b][:, :], weights(N_C + 3, (b * KW + k) * P), acts(first + k),
                                     k == 0, k == KW - 1)
                    last.then_inc(s_yp if b < 2 else s_used, 1)
                pe.wait_ge(s_acc, j * 2 + (KD + 2))
                pe.wait_ge(s_ab, j * 2 + (KD + 1))
                pe.wait_ge(s_row, j * 2 + 1)
                column(ps[3][:, 0:1], 1, 0)
                row(ps[4][:, 0:P], 1, 1).then_inc(s_red, 1)

            def token_product(n, k, t, first, last):
                for q in range(2):
                    ins = three(ps[2 * t + q][:, :], acts(k, t * P, (t + 1) * P), weights(n, q * 512, 512),
                                first, last)
                return ins

            for k in range(4):
                slab_ready(N_WO + k)
                pe.wait_ge(s_mlo, k + 1)
                for t in (0, 3, 2, 1):
                    if k == 0 and t == 0:
                        pe.wait_ge(s_sig, 3 * KD)
                    if k == 0 and t == 1:
                        pe.wait_ge(s_ab, 3 * KD)
                    if k == 0 and t == 2:
                        pe.wait_ge(s_row, 2 * KD)
                    if k == 0 and t == 3:
                        pe.wait_ge(s_y, 3 * KD)
                    last = token_product(N_WO + k, MERGED + k, t, k == 0, False)
                last.then_inc(s_used, 1)

            def x1_transpose(t):
                pe.wait_ge(s_x1n, t + 1)
                for q in range(2):
                    for i in range(4):
                        k = 4 * q + i
                        last = nc.tensor.transpose(ps[2 * t + q][:, i * P:(i + 1) * P],
                                                   x1n[t % 2][:, k * P:(k + 1) * P], ident[:, :])
                    last.then_inc(s_x1t, 1)

            for t in range(TT):
                for k in range(4, KD):
                    if t == 0:
                        slab_ready(N_WO + k)
                        pe.wait_ge(s_mlo, k + 1)
                    last = token_product(N_WO + k, MERGED + k, t, False, k == KD - 1)
                    if t == TT - 1:
                        last.then_inc(s_used, 1)
                    if t == 2 and k == 4:
                        x1_transpose(0)
                if t < TT - 1:
                    last.then_inc(s_wo, 1)
                if t == 2:
                    x1_transpose(1)

            pe.wait_ge(s_h2lo, 2)
            for i in range(4):
                project(N_UP + i, i, a=0, b=2 * P, used=False)
                if i in (0, 2):
                    x1_transpose(TT - 2 + i // 2)
            pe.wait_ge(s_h2lo, TT)
            for i in range(4):
                project(N_UP + i, i, a=2 * P, b=SEQ)
            with pe.Fori(1, KF // 2) as i:
                for f in range(2):
                    pe.wait_ge(s_a, i * 2 + (f - 1))
                    project(N_UP + 2 * f, 2 * f, it=i)
                    pe.wait_ge(s_g, i * 2 + (f - 1))
                    project(N_UP + 2 * f + 1, 2 * f + 1, it=i)

            for k in range(KF - 4):
                slab_ready(N_DOWN + k)
                for t in (2, 3, 0, 1):
                    if k == 0 and t == 0:
                        pe.wait_ge(s_a, KF)
                        pe.wait_ge(s_g, KF)
                    pe.wait_ge(s_glo, k + 1)
                    last = token_product(N_DOWN + k, k, t, k == 0, False)
                last.then_inc(s_used, 1)
            for t in range(TT - 1):
                for k in range(KF - 4, KF):
                    if t == 0:
                        slab_ready(N_DOWN + k)
                        pe.wait_ge(s_glo, k + 1)
                    last = token_product(N_DOWN + k, k, t, False, k == KF - 1)
                last.then_inc(s_dn, 1)
            t = TT - 1
            for q in range(2):
                for k in range(KF - 4, KF):
                    last = three(ps[2 * t + q][:, :], acts(k, t * P, SEQ), weights(N_DOWN + k, q * 512, 512),
                                 False, k == KF - 1)
                    if q == 1:
                        last.then_inc(s_used, 1)
                if q == 0:
                    last.then_inc(s_dn, 1)


_INS = ["x", "c", "w_mod", "b_mod", "g_mix", "w_in", "gm_ln_g", "gm_ln_b", "gm_w_s", "gm_b_s", "w_pa",
        "pool_w", "pool_scale", "w_pb", "conv_w", "w_pc", "w_o", "g_ffn", "w_13", "w_2", "g_final"]
_SQUEEZE = {"x", "w_mod", "w_in", "gm_w_s", "gm_b_s", "w_pa", "pool_w", "w_pb", "conv_w", "w_pc", "w_o",
            "w_13", "w_2"}


def kernel(**inputs):
    import numpy as np
    import concourse.bacc as bacc
    from concourse.bass_utils import run_bass_kernel_spmd

    nc = bacc.Bacc("TRN2", target_bir_lowering=False, num_devices=1, dynamic_dma_scratch_size=1024)
    arrays, args = {}, []
    for name in _INS:
        a = np.ascontiguousarray(inputs[name])
        if name in _SQUEEZE:
            a = a.reshape(a.shape[1:])
        arrays[f"in_{name}"] = a
        args.append(nc.dram_tensor(f"in_{name}", a.shape, mybir.dt.from_np(a.dtype), kind="ExternalInput").ap())
    out = nc.dram_tensor("out", (SEQ, D), fp32, kind="ExternalOutput").ap()
    build(nc, *args, out)
    r = run_bass_kernel_spmd(nc, [arrays], core_ids=[0])
    return r.results[0]["out"].reshape(1, SEQ, D)
```
